# Optimizing a Trainium2 kernel written in Bass

```python
import jax, jax.numpy as jnp
from jax import lax
import numpy as np
import functools

D_MODEL = 1024
BATCH = 1
SEQ = 256
DEPTH = 2

CHUNK = 64
GLA_HEADS = 4
GLA_DK = 64
GLA_DV = 128
GLA_RANK = 16
GLA_TAU = 16.0
RET_HEADS = 4
RET_DK = 128
RET_DV = 128
ROPE_BASE = 10000.0
D_FF = 2816
N_EXPERTS = 8
TOP_K = 2
D_FF_EXPERT = 1408
EPS = 1e-6
GLA_QK = GLA_HEADS * GLA_DK
GLA_V = GLA_HEADS * GLA_DV
RET_QK = RET_HEADS * RET_DK
RET_V = RET_HEADS * RET_DV
MIX_WIDTH = GLA_V + RET_V
IN_SPLITS = (GLA_QK, GLA_QK, GLA_V, GLA_V, GLA_RANK, RET_QK, RET_QK, RET_V, RET_V)
IN_WIDTH = sum(IN_SPLITS)
N_DENSE = (DEPTH + 1) // 2
N_MOE = DEPTH // 2


F32 = jnp.float32

def rms_norm(x, g):
    x32 = x.astype(F32)
    y = x32 * lax.rsqrt(jnp.mean(x32 * x32, axis=-1, keepdims=True) + EPS)
    return (y * g.astype(F32)).astype(x.dtype)

def to_chunks(t, n_heads):
    return t.reshape(t.shape[0], t.shape[1] // CHUNK, CHUNK, n_heads, -1)

def chunk_scan(decay, update):
    def step(state, inp):
        a, u = inp
        return a[..., None] * state + u, state
    init = jnp.zeros_like(update[:, 0])
    _, prev = lax.scan(step, init, (jnp.moveaxis(decay, 1, 0), jnp.moveaxis(update, 1, 0)))
    return jnp.moveaxis(prev, 0, 1)

def gla_core(q, k, v, log_a):
    b = jnp.cumsum(log_a, axis=2)
    b_last = b[:, :, -1:]
    eb, enb = jnp.exp(b), jnp.exp(-b)
    q_f, k_f = q * eb, k * enb
    q_b, k_b = q * enb, k * eb
    t_idx = jnp.arange(CHUNK)
    causal = t_idx[:, None] >= t_idx[None, :]
    s_fwd = jnp.einsum('bnthk,bnshk->bnhts', q_f, k_f)
    s_bwd = jnp.einsum('bnthk,bnshk->bnhts', q_b, k_b)
    scores = jnp.where(causal, s_fwd, s_bwd)
    o_intra = jnp.einsum('bnhts,bnshv->bnthv', scores, v)
    upd = jnp.einsum('bnshk,bnshv->bnhkv', k * jnp.exp(b_last - b), v)
    s_prev = chunk_scan(jnp.exp(b_last[:, :, 0]), upd)
    o_inter = jnp.einsum('bnthk,bnhkv->bnthv', q_f, s_prev)
    return o_intra + o_inter

def retention_core(q, k, v, log_gamma):
    t = jnp.arange(CHUNK, dtype=F32)
    dist = jnp.abs(t[:, None] - t[None, :])
    d_intra = jnp.exp(log_gamma[:, None, None] * dist)
    scores = jnp.einsum('bnthk,bnshk->bnhts', q, k) * d_intra
    o_intra = jnp.einsum('bnhts,bnshv->bnthv', scores, v)
    k_dec = k * jnp.exp(log_gamma[None, :] * (CHUNK - 1 - t)[:, None])[None, None, :, :, None]
    upd = jnp.einsum('bnshk,bnshv->bnhkv', k_dec, v)
    decay = jnp.broadcast_to(jnp.exp(log_gamma * CHUNK)[None, None, :, None], upd.shape[:-1])
    r_prev = chunk_scan(decay, upd)
    q_dec = q * jnp.exp(log_gamma[None, :] * (t + 1)[:, None])[None, None, :, :, None]
    o_inter = jnp.einsum('bnthk,bnhkv->bnthv', q_dec, r_prev)
    return o_intra + o_inter

def rotary(x, positions):
    half = x.shape[-1] // 2
    inv_freq = ROPE_BASE ** (-jnp.arange(half, dtype=F32) / half)
    ang = positions.astype(F32)[..., None] * inv_freq
    cos, sin = jnp.cos(ang)[:, :, None, :], jnp.sin(ang)[:, :, None, :]
    x1, x2 = x[..., :half], x[..., half:]
    return jnp.concatenate([x1 * cos - x2 * sin, x1 * sin + x2 * cos], axis=-1)

def hybrid_mixer(h, positions, w_in, w_alpha, b_alpha, gla_g, gn_g, gn_b, w_out):
    bsz, seq, _ = h.shape
    proj = (h @ w_in).astype(F32)
    gq, gk, gv, gr, ga, rq, rk, rv, rg = jnp.split(proj, np.cumsum(IN_SPLITS)[:-1], axis=-1)
    log_a = jax.nn.log_sigmoid(ga @ w_alpha.astype(F32) + b_alpha.astype(F32)) / GLA_TAU
    o_g = gla_core(to_chunks(gq * GLA_DK ** -0.5, GLA_HEADS), to_chunks(gk, GLA_HEADS),
                   to_chunks(gv, GLA_HEADS), to_chunks(log_a, GLA_HEADS))
    o_g = o_g.reshape(bsz, seq, GLA_HEADS, GLA_DV)
    o_g = o_g * lax.rsqrt(jnp.mean(o_g * o_g, axis=-1, keepdims=True) + EPS)
    o_g = o_g.reshape(bsz, seq, GLA_V) * gla_g.astype(F32) * jax.nn.silu(gr)
    log_gamma = jnp.log(1.0 - 2.0 ** (-5.0 - jnp.arange(RET_HEADS, dtype=F32)))
    rq = rotary(rq.reshape(bsz, seq, RET_HEADS, RET_DK), positions) * RET_DK ** -0.5
    rk = rotary(rk.reshape(bsz, seq, RET_HEADS, RET_DK), positions)
    o_r = retention_core(to_chunks(rq, RET_HEADS), to_chunks(rk, RET_HEADS),
                         to_chunks(rv, RET_HEADS), log_gamma)
    o_r = o_r.reshape(bsz, seq, RET_HEADS, RET_DV)
    mu = jnp.mean(o_r, axis=-1, keepdims=True)
    var = jnp.mean(jnp.square(o_r - mu), axis=-1, keepdims=True)
    o_r = ((o_r - mu) * lax.rsqrt(var + EPS)).reshape(bsz, seq, RET_V)
    o_r = (o_r * gn_g.astype(F32) + gn_b.astype(F32)) * jax.nn.silu(rg)
    o = jnp.concatenate([o_g, o_r], axis=-1).astype(h.dtype)
    return o @ w_out

def swiglu(h, w1, w3, w2):
    return (jax.nn.silu(h @ w1) * (h @ w3)) @ w2

def moe_swiglu(h, router_w, w1, w3, w2):
    logits = (h @ router_w).astype(F32)
    top_v, top_i = lax.top_k(logits, TOP_K)
    probs = jax.nn.softmax(top_v, axis=-1)
    gates = jnp.sum(jax.nn.one_hot(top_i, N_EXPERTS, dtype=F32) * probs[..., None], axis=-2)
    gates = gates.astype(h.dtype)
    out = jnp.zeros_like(h)
    for e in range(N_EXPERTS):
        out = out + gates[..., e:e + 1] * swiglu(h, w1[e], w3[e], w2[e])
    return out

def first_inputs(seed: int = 0) -> dict:
    key = jax.random.key(seed)
    ks = jax.random.split(key, 24)
    nrm = lambda k, shape, scale: jax.random.normal(k, shape, F32) * scale
    D = D_MODEL
    offsets = jax.random.randint(ks[2], (BATCH, 1), 0, 4096, dtype=jnp.int32)
    return {
        'x': nrm(ks[0], (BATCH, SEQ, D), 1.0),
        'c': nrm(ks[1], (BATCH, D), 1.0),
        'positions': offsets + jnp.arange(SEQ, dtype=jnp.int32)[None, :],
        'ada_w': nrm(ks[3], (DEPTH, D, 6 * D), 0.5 * D ** -0.5),
        'ada_b': nrm(ks[4], (DEPTH, 6 * D), 0.02),
        'norm_mix_g': 1.0 + nrm(ks[5], (DEPTH, D), 0.02),
        'norm_ffn_g': 1.0 + nrm(ks[6], (DEPTH, D), 0.02),
        'w_in': nrm(ks[7], (DEPTH, D, IN_WIDTH), D ** -0.5),
        'gla_w_alpha': nrm(ks[8], (DEPTH, GLA_RANK, GLA_QK), GLA_RANK ** -0.5),
        'gla_b_alpha': nrm(ks[9], (DEPTH, GLA_QK), 0.1),
        'gla_norm_g': 1.0 + nrm(ks[10], (DEPTH, GLA_V), 0.02),
        'ret_gn_g': 1.0 + nrm(ks[11], (DEPTH, RET_V), 0.02),
        'ret_gn_b': nrm(ks[12], (DEPTH, RET_V), 0.02),
        'w_out': nrm(ks[13], (DEPTH, MIX_WIDTH, D), MIX_WIDTH ** -0.5),
        'ffn_w1': nrm(ks[14], (N_DENSE, D, D_FF), D ** -0.5),
        'ffn_w3': nrm(ks[15], (N_DENSE, D, D_FF), D ** -0.5),
        'ffn_w2': nrm(ks[16], (N_DENSE, D_FF, D), D_FF ** -0.5),
        'router_w': nrm(ks[17], (N_MOE, D, N_EXPERTS), D ** -0.5),
        'moe_w1': nrm(ks[18], (N_MOE, N_EXPERTS, D, D_FF_EXPERT), D ** -0.5),
        'moe_w3': nrm(ks[19], (N_MOE, N_EXPERTS, D, D_FF_EXPERT), D ** -0.5),
        'moe_w2': nrm(ks[20], (N_MOE, N_EXPERTS, D_FF_EXPERT, D), D_FF_EXPERT ** -0.5),
        'final_g': 1.0 + nrm(ks[21], (D,), 0.02),
    }

def first_block(x, c, positions, ada_w, ada_b, norm_mix_g, norm_ffn_g, w_in, gla_w_alpha,
              gla_b_alpha, gla_norm_g, ret_gn_g, ret_gn_b, w_out, ffn_w1, ffn_w3, ffn_w2,
              router_w, moe_w1, moe_w3, moe_w2, final_g):
    cond = jax.nn.silu(c)
    for layer in range(DEPTH):
        mod = (cond @ ada_w[layer] + ada_b[layer])[:, None, :]
        sh1, sc1, g1, sh2, sc2, g2 = jnp.split(mod, 6, axis=-1)
        h = rms_norm(x, norm_mix_g[layer]) * (1.0 + sc1) + sh1
        x = x + g1 * hybrid_mixer(h, positions, w_in[layer], gla_w_alpha[layer],
                                  gla_b_alpha[layer], gla_norm_g[layer], ret_gn_g[layer],
                                  ret_gn_b[layer], w_out[layer])
        h = rms_norm(x, norm_ffn_g[layer]) * (1.0 + sc2) + sh2
        i = layer // 2
        if layer % 2 == 0:
            y = swiglu(h, ffn_w1[i], ffn_w3[i], ffn_w2[i])
        else:
            y = moe_swiglu(h, router_w[i], moe_w1[i], moe_w3[i], moe_w2[i])
        x = x + g2 * y
    return rms_norm(x, final_g)


GRID_W = 64
CTX_LEN = 256
N_MIXERS = 2
N_A = (DEPTH + 1) // 2
N_B = DEPTH // 2
N_MOD = 9
CONV_DIM = D_MODEL
CONV_W = 3
MLA_HEADS = 8
QK_NOPE = 128
QK_ROPE = 64
QK_HEAD = QK_NOPE + QK_ROPE
V_HEAD = 128
Q_LORA = 256
KV_LORA = 128
QK_SCALE = QK_HEAD ** -0.5
Q_BLOCK = 128


def rms_norm_2(x, g):
    xf = x.astype(jnp.float32)
    y = xf * lax.rsqrt(jnp.mean(xf * xf, axis=-1, keepdims=True) + EPS)
    return (y * g.astype(jnp.float32)).astype(x.dtype)

def adaln_chunks(cond, w_mod, b_mod):
    m = jax.nn.silu(cond) @ w_mod + b_mod
    return jnp.split(m[:, None, :], N_MOD, axis=-1)

def pre(h, g, shift, scale):
    return rms_norm_2(h, g) * (1 + scale) + shift

def swiglu_2(h, w1, w3, w2):
    return (jax.nn.silu(h @ w1) * (h @ w3)) @ w2

def conv3_centred(u, w):
    return lax.conv_general_dilated(
        u, w[:, None, :].astype(u.dtype), window_strides=(1,), padding=((1, 1),),
        dimension_numbers=("NWC", "WIO", "NWC"), feature_group_count=u.shape[-1])

def short_conv_mixer(h, w_in, conv_w, w_out):
    b_gate, c_gate, u = jnp.split(h @ w_in, 3, axis=-1)
    return (b_gate * conv3_centred(c_gate * u, conv_w)) @ w_out

def axial_rope_tables(n):
    rows = n // GRID_W
    r = jnp.broadcast_to(jnp.arange(rows)[:, None], (rows, GRID_W)).reshape(n).astype(jnp.float32)
    col = jnp.broadcast_to(jnp.arange(GRID_W)[None, :], (rows, GRID_W)).reshape(n).astype(jnp.float32)
    n_freq = QK_ROPE // 4
    inv = ROPE_BASE ** (-jnp.arange(n_freq, dtype=jnp.float32) / n_freq)
    ang = jnp.stack([r[:, None] * inv, col[:, None] * inv], axis=1)
    return jnp.cos(ang), jnp.sin(ang)

def apply_axial_rope(t, cos, sin):
    ts = t.reshape(t.shape[:-1] + (2, 2, QK_ROPE // 4))
    x1, x2 = ts[..., 0, :], ts[..., 1, :]
    cos = cos.astype(t.dtype)
    sin = sin.astype(t.dtype)
    y = jnp.stack([x1 * cos - x2 * sin, x1 * sin + x2 * cos], axis=-2)
    return y.reshape(t.shape)

def rope_tail(t, cos, sin):
    return jnp.concatenate([t[..., :QK_NOPE], apply_axial_rope(t[..., QK_NOPE:], cos, sin)], axis=-1)

def mla_down(h, w_a):
    return jnp.split(h @ w_a, [Q_LORA, Q_LORA + KV_LORA], axis=-1)

def mla_queries(cq, g_qa, w_uq, g_q):
    b, n, _ = cq.shape
    q = (rms_norm_2(cq, g_qa) @ w_uq).reshape(b, n, MLA_HEADS, QK_HEAD)
    return rms_norm_2(q, g_q).transpose(0, 2, 1, 3)

def mla_keys_values(ckv, k_rope, g_kva, w_ukv, g_k):
    b, n, _ = ckv.shape
    kv = (rms_norm_2(ckv, g_kva) @ w_ukv).reshape(b, n, MLA_HEADS, QK_NOPE + V_HEAD)
    k_nope, v = jnp.split(kv, [QK_NOPE], axis=-1)
    k_r = jnp.broadcast_to(k_rope[:, :, None, :], (b, n, MLA_HEADS, QK_ROPE))
    k = rms_norm_2(jnp.concatenate([k_nope, k_r], axis=-1), g_k)
    return k.transpose(0, 2, 1, 3), v.transpose(0, 2, 1, 3)

def softmax_attend(q, k, v):
    s = jnp.einsum("bhqd,bhkd->bhqk", q, k).astype(jnp.float32) * QK_SCALE
    p = jax.nn.softmax(s, axis=-1).astype(v.dtype)
    return jnp.einsum("bhqk,bhkd->bhqd", p, v)

def merge_heads(o):
    b, h, n, d = o.shape
    return o.transpose(0, 2, 1, 3).reshape(b, n, h * d)

def latent_attention(q, k_all, v_all):
    b, h, n, dq = q.shape
    nb = n // Q_BLOCK
    qb = q.reshape(b, h, nb, Q_BLOCK, dq).transpose(2, 0, 1, 3, 4)
    o = lax.map(lambda qblk: softmax_attend(qblk, k_all, v_all), qb)
    return o.transpose(1, 0, 3, 2, 4).reshape(b, n, h * V_HEAD)

def second_inputs(seed: int = 0) -> dict:
    key = jax.random.key(seed)
    ks = jax.random.split(key, 24)
    f32 = jnp.float32

    def nrm(k, shape, scale):
        return jax.random.normal(k, shape, f32) * scale

    def gain(k, shape):
        return 1.0 + 0.1 * jax.random.normal(k, shape, f32)

    D = D_MODEL
    return {
        "x": nrm(ks[0], (BATCH, SEQ, D), 1.0),
        "c": nrm(ks[1], (BATCH, D), 1.0),
        "ctx": nrm(ks[2], (BATCH, CTX_LEN, D), 1.0),
        "c_ctx": nrm(ks[3], (D,), 1.0),
        "w_mod": nrm(ks[4], (DEPTH, D, N_MOD * D), 0.5 * D ** -0.5),
        "b_mod": nrm(ks[5], (DEPTH, N_MOD * D), 0.02),
        "g_norm": gain(ks[6], (DEPTH, 3, D)),
        "ffn_w1": nrm(ks[7], (DEPTH, 2, D, D_FF), D ** -0.5),
        "ffn_w3": nrm(ks[8], (DEPTH, 2, D, D_FF), D ** -0.5),
        "ffn_w2": nrm(ks[9], (DEPTH, 2, D_FF, D), D_FF ** -0.5),
        "sc_w_in": nrm(ks[10], (N_A, D, 3 * CONV_DIM), D ** -0.5),
        "sc_conv": nrm(ks[11], (N_A, CONV_W, CONV_DIM), CONV_W ** -0.5),
        "sc_w_out": nrm(ks[12], (N_A, CONV_DIM, D), CONV_DIM ** -0.5),
        "mla_w_a": nrm(ks[13], (N_B, D, Q_LORA + KV_LORA + QK_ROPE), D ** -0.5),
        "mla_g_qa": gain(ks[14], (N_B, Q_LORA)),
        "mla_w_uq": nrm(ks[15], (N_B, Q_LORA, MLA_HEADS * QK_HEAD), Q_LORA ** -0.5),
        "mla_g_kva": gain(ks[16], (N_B, KV_LORA)),
        "mla_w_ukv": nrm(ks[17], (N_B, KV_LORA, MLA_HEADS * (QK_NOPE + V_HEAD)), KV_LORA ** -0.5),
        "mla_g_q": gain(ks[18], (N_B, QK_HEAD)),
        "mla_g_k": gain(ks[19], (N_B, QK_HEAD)),
        "mla_w_o": nrm(ks[20], (N_B, MLA_HEADS * V_HEAD, D), (MLA_HEADS * V_HEAD) ** -0.5),
    }

def second_block(x, c, ctx, c_ctx, w_mod, b_mod, g_norm, ffn_w1, ffn_w3, ffn_w2,
              sc_w_in, sc_conv, sc_w_out, mla_w_a, mla_g_qa, mla_w_uq, mla_g_kva,
              mla_w_ukv, mla_g_q, mla_g_k, mla_w_o):
    n = x.shape[1]
    cos, sin = axial_rope_tables(n)
    h_x, h_c = x, ctx
    for i in range(DEPTH):
        kind, j = i % N_MIXERS, i // N_MIXERS
        last = i == DEPTH - 1
        run_ctx_in = (not last) or kind == 1
        run_ctx_out = not last

        mx = adaln_chunks(c, w_mod[i], b_mod[i])
        mc = adaln_chunks(c_ctx[None], w_mod[i], b_mod[i])
        ffn1 = functools.partial(swiglu_2, w1=ffn_w1[i, 0], w3=ffn_w3[i, 0], w2=ffn_w2[i, 0])
        ffn2 = functools.partial(swiglu_2, w1=ffn_w1[i, 1], w3=ffn_w3[i, 1], w2=ffn_w2[i, 1])

        h_x = h_x + 0.5 * mx[2] * ffn1(pre(h_x, g_norm[i, 0], mx[0], mx[1]))
        if run_ctx_in:
            h_c = h_c + 0.5 * mc[2] * ffn1(pre(h_c, g_norm[i, 0], mc[0], mc[1]))

        nx = pre(h_x, g_norm[i, 1], mx[3], mx[4])
        if kind == 0:
            ox = short_conv_mixer(nx, sc_w_in[j], sc_conv[j], sc_w_out[j])
            if run_ctx_out:
                nc = pre(h_c, g_norm[i, 1], mc[3], mc[4])
                oc = short_conv_mixer(nc, sc_w_in[j], sc_conv[j], sc_w_out[j])
        else:
            nc = pre(h_c, g_norm[i, 1], mc[3], mc[4])
            cq_c, ckv_c, kr_c = mla_down(nc, mla_w_a[j])
            k_c, v_c = mla_keys_values(ckv_c, kr_c, mla_g_kva[j], mla_w_ukv[j], mla_g_k[j])
            cq_x, ckv_x, kr_x = mla_down(nx, mla_w_a[j])
            k_x, v_x = mla_keys_values(ckv_x, kr_x, mla_g_kva[j], mla_w_ukv[j], mla_g_k[j])
            k_x = rope_tail(k_x, cos, sin)
            q_x = rope_tail(mla_queries(cq_x, mla_g_qa[j], mla_w_uq[j], mla_g_q[j]), cos, sin)
            k_all = jnp.concatenate([k_c, k_x], axis=2)
            v_all = jnp.concatenate([v_c, v_x], axis=2)
            ox = latent_attention(q_x, k_all, v_all) @ mla_w_o[j]
            if run_ctx_out:
                q_c = mla_queries(cq_c, mla_g_qa[j], mla_w_uq[j], mla_g_q[j])
                oc = merge_heads(softmax_attend(q_c, k_c, v_c)) @ mla_w_o[j]
        h_x = h_x + mx[5] * ox
        if run_ctx_out:
            h_c = h_c + mc[5] * oc

        h_x = h_x + 0.5 * mx[8] * ffn2(pre(h_x, g_norm[i, 2], mx[6], mx[7]))
        if run_ctx_out:
            h_c = h_c + 0.5 * mc[8] * ffn2(pre(h_c, g_norm[i, 2], mc[6], mc[7]))
    return h_x


def setup_inputs(seed=0):
    out = dict(first_inputs(seed))
    for name, value in second_inputs(seed + 1).items():
        if name != "x":
            out[name + "_2"] = value
    return out


def reference(
    x, c, positions, ada_w, ada_b, norm_mix_g, norm_ffn_g, w_in, gla_w_alpha, gla_b_alpha,
    gla_norm_g, ret_gn_g, ret_gn_b, w_out, ffn_w1, ffn_w3, ffn_w2, router_w, moe_w1, moe_w3,
    moe_w2, final_g, c_2, ctx_2, c_ctx_2, w_mod_2, b_mod_2, g_norm_2, ffn_w1_2, ffn_w3_2,
    ffn_w2_2, sc_w_in_2, sc_conv_2, sc_w_out_2, mla_w_a_2, mla_g_qa_2, mla_w_uq_2, mla_g_kva_2,
    mla_w_ukv_2, mla_g_q_2, mla_g_k_2, mla_w_o_2,
):
    x = first_block(
        x, c, positions, ada_w, ada_b, norm_mix_g, norm_ffn_g, w_in, gla_w_alpha, gla_b_alpha,
        gla_norm_g, ret_gn_g, ret_gn_b, w_out, ffn_w1, ffn_w3, ffn_w2, router_w, moe_w1, moe_w3,
        moe_w2, final_g,
    )
    return second_block(
        x, c_2, ctx_2, c_ctx_2, w_mod_2, b_mod_2, g_norm_2, ffn_w1_2, ffn_w3_2, ffn_w2_2,
        sc_w_in_2, sc_conv_2, sc_w_out_2, mla_w_a_2, mla_g_qa_2, mla_w_uq_2, mla_g_kva_2,
        mla_w_ukv_2, mla_g_q_2, mla_g_k_2, mla_w_o_2,
    )


_drawn_inputs = setup_inputs


def setup_inputs(seed=0):
    import zlib

    import numpy as np

    out = dict(_drawn_inputs(seed))
    spreads = {}
    factors = {'norm_mix_g': 3.217,
     'norm_ffn_g': 2.972,
     'gla_b_alpha': 4.737,
     'gla_norm_g': 8.0,
     'ret_gn_g': 4.397,
     'ret_gn_b': 4.259,
     'ctx_2': 4.111,
     'mla_g_qa_2': 8.0,
     'mla_g_kva_2': 6.75,
     'mla_g_q_2': 8.0,
     'mla_g_k_2': 8.0}
    for name, (base, spread) in spreads.items():
        noise = np.random.default_rng([zlib.crc32(name.encode()), seed]).standard_normal(out[name].shape)
        drawn = base * np.exp(spread * noise) if base else spread * noise
        out[name] = __import__('jax').numpy.asarray(drawn.astype(out[name].dtype))
    for name, factor in factors.items():
        out[name] = (out[name] * factor).astype(out[name].dtype)
    return out
```

```python
from contextlib import ExitStack

import numpy as np

import concourse.bass as bass
from concourse import mybir

F32 = mybir.dt.float32
F32R = mybir.dt.float32r
I32 = mybir.dt.int32
U32 = mybir.dt.uint32
ALU = mybir.AluOpType
ACT = mybir.ActivationFunctionType
AX = mybir.AxisListType

PART = 128
D = 1024
KD = D // PART
SEQ = 256
CTX = 256
BOTH = SEQ + CTX
EPS = 1e-6
HALF_F = 1408
UNITS = HALF_F // PART
N_EXPERTS = 8
CHUNK = 64
HEADS = 4
GLA_DK = 64
GLA_TAU = 16.0
RET_DK = 128
RANK = 16
MLA_HEADS = 8
QK_HEAD = 192
Q_LORA = 256
QK_SCALE = QK_HEAD ** -0.5

PANEL = 11
SLOTS = 4
USED0 = 1
AHEAD = 3
EXPERT_PANELS = (2 * UNITS * KD + UNITS * KD) // PANEL
EXPERT_GROUPS = UNITS + KD // 2
ADA_SLOTS = 3
ADA_FIRST = 18
ADA1, ADA2 = 6 * KD, 9 * KD

PHASES = [
    ("win0", 28, 12), ("wout0", 8, 4), ("dense", 2 * EXPERT_PANELS, 2 * EXPERT_GROUPS),
    ("win1", 28, 12), ("wout1", 8, 4), ("moe", N_EXPERTS * EXPERT_PANELS, N_EXPERTS * EXPERT_GROUPS),
    ("ffn00", 2 * EXPERT_PANELS, 2 * EXPERT_GROUPS), ("conv_cu", 16, 8), ("conv_b", 8, 4), ("conv_out", 8, 4),
    ("ffn01", 2 * EXPERT_PANELS, 2 * EXPERT_GROUPS), ("ffn10", 2 * EXPERT_PANELS, 2 * EXPERT_GROUPS),
    ("mla", 9, 13), ("mla_o", 8, 4), ("ffn11", 2 * EXPERT_PANELS, 2 * EXPERT_GROUPS),
]
P0, G0 = {}, {}
_p, _g = 0, 2
for _name, _np, _ng in PHASES:
    P0[_name], G0[_name] = _p, _g
    _p, _g = _p + _np, _g + _ng
PANELS = -(-(_p + AHEAD) // SLOTS) * SLOTS
NARROW = [q for n, c, _ in PHASES if c < EXPERT_PANELS + 5 for q in range(P0[n], P0[n] + c)]


def width(q):
    return (KD if q in NARROW else PANEL) * PART


SET0 = {"wout0": 1, "dense": 2, "wout1": 4, "moe": 5, "ffn00": 14, "conv_out": 16, "ffn01": 17, "ffn10": 19, "mla_o": 21}
NORM_SET = (0, 1, 3, 4, 12, 13, 15, 16, 18, 20, 21)
NORM_OF = ("win0", "dense", "win1", "moe", "ffn00", "ffn00", "conv_cu", "ffn01", "ffn10", "mla", "ffn11")
P0["end"], G0["end"] = _p, _g

VEC = {}
_v = 0
for _name, _n in [("mix_g", 16), ("ffn_g", 16), ("ada_b", 96), ("mod_b", 144),
                  ("g2", 48), ("alpha_b", 4), ("gla_g", 8), ("gn_g", 8), ("gn_b", 8), ("final_g", 8),
                  ("conv", 24), ("qa_g", 2), ("kva_g", 1), ("q_g", 2), ("k_g", 2)]:
    VEC[_name] = (_v, _n)
    _v += _n
VECS = _v


def gammas():
    return 1.0 - 2.0 ** (-5.0 - np.arange(HEADS, dtype=np.float64))


def constants():
    t = np.arange(PART)
    same = (t[:, None] // CHUNK) == (t[None, :] // CHUNK)
    g = gammas()
    lg = np.log(g)
    out = {"ident": np.eye(PART), "ones": np.ones((PART, PART))}
    out["causal"] = same & (t[None, :] >= t[:, None])
    out["anti"] = same & (t[None, :] < t[:, None])
    dist = np.abs(t[:, None] - t[None, :])
    out["ret_decay"] = np.concatenate(
        [np.where(same, np.exp(lg[h] * dist), 0.0) * RET_DK ** -0.5 for h in range(HEADS)], axis=1)
    out["ret_k"] = np.exp(lg[None, :] * (CHUNK - 1 - t % CHUNK)[:, None])
    qd = np.concatenate([np.exp(lg[h] * (np.arange(CHUNK) + 1)) * RET_DK ** -0.5 for h in range(HEADS)])
    out["ret_q"] = np.broadcast_to(qd[None, :], (PART, HEADS * CHUNK))
    half = RET_DK // 2
    inv = 10000.0 ** (-np.arange(half) / half)
    out["inv_freq"] = np.concatenate([inv, inv])[:, None]
    turn = np.zeros((PART, PART))
    turn[np.arange(half) + half, np.arange(half)] = -1.0
    turn[np.arange(half), np.arange(half) + half] = 1.0
    out["turn"] = turn
    nf = 16
    inv2 = (10000.0 ** (-np.arange(nf) / nf)).astype(np.float32)
    pos = np.arange(SEQ)
    row, col = (pos // 64).astype(np.float32), (pos % 64).astype(np.float32)
    r = t % 64
    ang = np.where((r // 32 == 0)[:, None], row[None, :], col[None, :]).astype(np.float32) * inv2[r % 16][:, None]
    out["ax_cos"], out["ax_sin"] = np.cos(ang.astype(np.float64)), np.sin(ang.astype(np.float64))
    ax = np.zeros((PART, PART))
    for m in range(PART):
        if m % 32 < 16:
            ax[m + 16, m] = -1.0
        else:
            ax[m - 16, m] = 1.0
    out["ax_turn"] = ax
    for i, name in enumerate(("low", "high")):
        out[name] = (t // 64 == i)[:, None]
    out["iota"] = np.broadcast_to(np.arange(N_EXPERTS)[None, :], (PART, N_EXPERTS))
    return {n: np.ascontiguousarray(a, dtype=np.float32) for n, a in out.items()}


CONST = {}
_c = 0
for _name, _a in constants().items():
    CONST[_name] = (_c, _a.shape[1])
    _c += _a.shape[1]
CONSTS = _c

TWO_PI = 2.0 * np.pi
PI_HI = float(np.float32(6.28125))
PI_MID = float(np.float32(TWO_PI - PI_HI))
PI_LO = float(np.float32(TWO_PI - PI_HI - PI_MID))
ROUND = float(1.5 * 2 ** 23)
PI_MAX = float(np.nextafter(np.float32(np.pi), np.float32(0)))


def build(nc, wstream, adastream, c_rows, vecs, consts, xT, ctxT, pos, w_ga, w_alpha, router, out, last="end"):
    ctx = ExitStack()
    with ctx:
        def sb(name, shape, dt=F32, stack=ctx):
            return stack.enter_context(nc.sbuf_tensor(name, shape, dt))

        def sem(name):
            return ctx.enter_context(nc.semaphore(name))

        raw = sb("raw", [PART, SLOTS, PANEL * PART])
        whi = sb("whi", [PART, SLOTS, PANEL * PART], F32R)
        wlo = sb("wlo", [PART, SLOTS, PANEL * PART], F32R)
        with ExitStack() as s:
            cq_hi = sb("cq_hi", [PART, 2, SEQ], F32R, s)
            cq_lo = sb("cq_lo", [PART, 2, SEQ], F32R, s)
            ckv_hi = sb("ckv_hi", [PART, BOTH], F32R, s)
            ckv_lo = sb("ckv_lo", [PART, BOTH], F32R, s)
        ada = sb("ada", [PART, ADA_SLOTS, D])
        cond = sb("cond", [PART, 2, D])
        X = sb("X", [PART, KD, BOTH])
        stage_a = sb("stage_a", [PART, 2, BOTH])
        stage_b = sb("stage_b", [PART, 2, BOTH])
        vec = sb("vec", [PART, VECS])
        con = sb("con", [PART, CONSTS])
        mod1 = sb("mod1", [PART, 2, 48])
        mod2 = sb("mod2", [PART, 2, 72, 2])
        amp1 = sb("amp1", [PART, 2, 2, KD])
        amp2 = sb("amp2", [PART, 2, 3, KD, 2])
        gate2 = sb("gate2", [PART, 2, 3, KD, 2])
        wga = sb("wga", [PART, 2, KD, RANK])
        walpha = sb("walpha", [RANK, 2, 2 * PART])
        wroute = sb("wroute", [PART, KD, N_EXPERTS])
        ms = sb("ms", [PART, 36])
        root = sb("root", [PART, 32])
        rstd = sb("rstd", [PART, 32])
        zc0 = sb("zc0", [PART, 2])
        trig = sb("trig", [PART, 2, SEQ])
        h_hi, h_lo, hid_hi, hid_lo = {}, {}, {}, {}
        with ExitStack() as s:
            h_hi[BOTH] = sb("h_hi", [PART, KD, BOTH], F32R, s)
            h_lo[BOTH] = sb("h_lo", [PART, KD, BOTH], F32R, s)
            with ExitStack() as s2:
                hid_hi[BOTH] = sb("hid_hi", [PART, UNITS, BOTH], F32R, s2)
                hid_lo[BOTH] = sb("hid_lo", [PART, UNITS, BOTH], F32R, s2)
            with ExitStack() as s2:
                zc = sb("zc", [PART, KD, 2, SEQ + 2], F32, s2)
                y_hi = sb("y_hi", [PART, KD, BOTH], F32R, s2)
                y_lo = sb("y_lo", [PART, KD, BOTH], F32R, s2)
            with ExitStack() as s2:
                kn = sb("kn", [PART, MLA_HEADS, BOTH], F32, s2)
                krt = sb("krt", [PART, MLA_HEADS // 2, BOTH], F32, s2)
                qr = sb("qr", [PART, MLA_HEADS // 2, SEQ], F32, s2)
                val2 = sb("val2", [PART, 4, MLA_HEADS * PART], F32, s2)
        with ExitStack() as s:
            h_hi[SEQ] = sb("h_hi1", [PART, KD, SEQ], F32R, s)
            h_lo[SEQ] = sb("h_lo1", [PART, KD, SEQ], F32R, s)
            with ExitStack() as s2:
                hid_hi[SEQ] = sb("hid_hi1", [PART, UNITS, SEQ], F32R, s2)
                hid_lo[SEQ] = sb("hid_lo1", [PART, UNITS, SEQ], F32R, s2)
                gates = sb("gates", [PART, N_EXPERTS, SEQ], F32, s2)
                gdiag = sb("gdiag", [PART, 2, N_EXPERTS, PART], F32, s2)
                gated = sb("gated", [PART, 2, SEQ], F32, s2)
                gt = sb("gt", [PART, 2, 64], F32, s2)
                gi = sb("gi", [PART, 2, 8], U32, s2)
            with ExitStack() as s2:
                mix = sb("mix", [PART, 16400], F32, s2)
            with ExitStack() as s2:
                late = sb("late", [PART, 4096], F32, s2)
        with ExitStack() as s:
            angles_in = sb("angles_in", [PART, 4, SEQ], F32, s)
            ada_first = sb("ada_first", [PART, ADA_FIRST, D], F32, s)
        PS = ctx.enter_context(nc.psum_tensor("PS", [PART, 8, 512], F32))
        BC_BANK = 7
        SUMS = 0
        diag = stage_b[:, 1, :].rearrange("p (a b) -> p a b", a=4)

        def V(name, i, n=1):
            return vec[:, VEC[name][0] + i:VEC[name][0] + i + n]

        def C(name):
            return con[:, CONST[name][0]:CONST[name][0] + CONST[name][1]]

        ident, ones = C("ident"), C("ones")

        def carve(big, at, sizes):
            views = {}
            for name, shape in sizes:
                n = int(np.prod(shape))
                v = big[:, at:at + n]
                if len(shape) == 2:
                    v = v.rearrange("p (a b) -> p a b", a=shape[0])
                if len(shape) == 3:
                    v = v.rearrange("p (a b c) -> p a b c", a=shape[0], b=shape[1])
                views[name] = v
                at += n
            return views, at

        m, at = carve(mix, 0, [("prj", (20, SEQ)), ("val", (2, 1024))])
        MX_A = at
        a, at = carve(mix, MX_A, [("zb", (2, SEQ)), ("ln", (2, SEQ)), ("cum_a", (2, SEQ)), ("cum_b", (2, SEQ)),
                                  ("eb", (2, SEQ)), ("enb", (2, SEQ)), ("ekd", (2, SEQ))])
        m.update(a)
        m["kd"], m["kb"], m["qb"], m["ga"] = m["zb"], m["ln"], m["cum_b"], m["ekd"][0:RANK, 0, :]
        m.update(carve(mix, MX_A, [("odiag", (16, PART))])[0])
        MX_B = at
        b, at = carve(mix, MX_B, [("sc", (2, 512)), ("kdt", (4, PART)), ("kdr", (2, 512)),
                                  ("gs", (3, HEADS, PART)), ("rs", (3, 512))])
        m.update(b)
        m["sr"] = stage_a
        m.update(carve(mix, MX_B, [("t1", (4, SEQ)), ("t2", (4, SEQ))])[0])
        m.update(carve(mix, MX_B, [("o", (8, SEQ)), ("osq", (8, SEQ))])[0])
        pts = late[:, 0:2048].rearrange("p (n k q) -> p n k q", n=2, k=4)
        probs = late[:, 2048:4096].rearrange("p (n t k) -> p n t k", n=2, t=2)
        SCORE_BANK = (0, 6)
        posi, angle, turns, red = (angles_in[:, i, :] for i in range(4))

        x_in, ctx_in, small_in, pos_in = sem("x_in"), sem("ctx_in"), sem("small_in"), sem("pos_in")
        raw_in = [sem(f"raw_in{i}") for i in range(SLOTS)]
        ada_in = [sem(f"ada_in{i}") for i in range(ADA_SLOTS)]
        hi_split, lo_split = sem("hi_split"), sem("lo_split")
        panel_used = sem("panel_used")
        ada_first_in = [sem(f"ada_first_in{i}") for i in range(6)]
        ada_done = sem("ada_done")
        unit_done, group_done = sem("unit_done"), sem("group_done")
        evacuated = sem("evacuated")
        silu_done, hid_hi_done, hid_ready = sem("silu_done"), sem("hid_hi_done"), sem("hid_ready")
        cond_in, cond2_in, cond_ready = sem("cond_in"), sem("cond2_in"), sem("cond_ready")
        sq_done, acc_done = sem("sq_done"), sem("acc_done")
        sumsq_ready, ms_ready, root_ready = sem("sumsq_ready"), sem("ms_ready"), sem("root_ready")
        diag_ready, bc_ready = sem("diag_ready"), sem("bc_ready")
        xhat_ready, h_hi_ready, h_ready = sem("xhat_ready"), sem("h_hi_ready"), sem("h_ready")
        dve_step, act_step = sem("dve_step"), sem("act_step")
        final_ready, out_done = sem("final_ready"), sem("out_done")
        named = {}

        def S(name):
            if name not in named:
                named[name] = sem(name)
            return named[name]

        def halves(T):
            return [(0, SEQ, 0)] + ([(SEQ, BOTH, 1)] if T == BOTH else [])

        def norm1(layer, which):
            return (SEQ, lambda c, s: amp1[:, layer, which, c:c + 1],
                    lambda c, s: mod1[:, layer, 24 * which + c:24 * which + c + 1])

        def norm2(layer, which, T):
            return (T, lambda c, s: amp2[:, layer, which, c, s:s + 1],
                    lambda c, s: mod2[:, layer, 24 * which + c, s:s + 1])

        FINAL1 = 4
        NORMS = [norm1(0, 0), norm1(0, 1), norm1(1, 0), norm1(1, 1), (SEQ, None, None),
                 norm2(0, 0, BOTH), norm2(0, 1, BOTH), norm2(0, 2, BOTH),
                 norm2(1, 0, BOTH), norm2(1, 1, BOTH), norm2(1, 2, SEQ)]

        def modulated(n):
            return n if n <= FINAL1 else n - 1

        FFN = {"dense": (0, 2, SEQ, (ADA1, 15)), "moe": (2, 8, SEQ, (2 * ADA1, 3)),
               "ffn00": (10, 2, BOTH, (2 * ADA1 + 3 * KD, 3 * KD)), "ffn01": (12, 2, BOTH, (2 * ADA1 + ADA2, 18)),
               "ffn10": (14, 2, BOTH, (2 * ADA1 + ADA2 + 36, 18)), "ffn11": (16, 2, SEQ, None)}
        ORDER = [n for n, _, _ in PHASES]

        def runs(name):
            return last == "end" or ORDER.index(name) < ORDER.index(last)

        n_panels = P0[last] + AHEAD
        n_rounds = -(-n_panels // SLOTS)
        n_ada1 = (ADA1 - ADA_FIRST + 30 * runs("dense") + 18 * runs("win1")) // ADA_SLOTS
        n_ada2 = sum(FFN[n][1] * FFN[n][3][1] for n in ("moe", "ffn00", "ffn01", "ffn10") if runs(n)) // ADA_SLOTS
        rounds = []
        for r in range(n_rounds):
            w = max(width(q) for q in range(SLOTS * r, SLOTS * r + SLOTS))
            if r > 1 and rounds[-1][2] == w:
                rounds[-1] = (rounds[-1][0], r + 1, w)
            else:
                rounds.append((r, r + 1, w))

        block = ctx.enter_context(nc.Block())

        @block.sync
        def _(sp):
            sp.dma_start(X[:, :, 0:SEQ], xT).then_inc(x_in, 16)
            sp.dma_start(vec[:, :], vecs).then_inc(small_in, 16)
            sp.dma_start(con[:, :], consts).then_inc(small_in, 16)
            sp.dma_start(wga[:, :, :, :], w_ga).then_inc(small_in, 16)
            sp.dma_start(walpha[:, :, :], w_alpha).then_inc(small_in, 16)
            sp.dma_start(wroute[:, :, :], router).then_inc(small_in, 16)
            sp.dma_start(posi.bitcast(I32), pos).then_inc(small_in, 16)
            sp.wait_ge(ada_first_in[1], 16)
            for j in range(SLOTS):
                sp.dma_start(raw[:, j, 0:width(j)], wstream[j, :, 0:width(j)]).then_inc(raw_in[j], 16)
            sp.wait_ge(ada_first_in[5], 16)
            sp.dma_start(X[:, :, SEQ:BOTH], ctxT).then_inc(ctx_in, 16)
            for first, end, w in rounds[1:]:
                with nc.sync.Fori(first, end) as r:
                    for j in range(SLOTS):
                        sp.wait_ge(lo_split, SLOTS * r - SLOTS + j + 1)
                        src = wstream[bass.ds(SLOTS * r + j, 1), :, 0:w].rearrange("a p n -> p (a n)")
                        sp.dma_start(raw[:, j, 0:w], src).then_inc(raw_in[j], 16)
            for j in range(SLOTS):
                sp.wait_ge(raw_in[j], 16 * n_rounds)
            sp.wait_ge(evacuated, G0[last])
            sp.dma_start(out, X[:, :, 0:SEQ]).then_inc(out_done, 16)
            sp.wait_ge(out_done, 16)

        @block.gpsimd
        def _(pool):
            pool.wait_ge(ada_first_in[3], 16)
            for j in range(ADA_SLOTS):
                pool.dma_start(ada[:, j, :], adastream[ADA_FIRST + j]).then_inc(ada_in[j], 16)
            with nc.gpsimd.Fori(1, n_ada1) as r:
                for j in range(ADA_SLOTS):
                    pool.wait_ge(ada_done, ADA_SLOTS * r + (ADA_FIRST - ADA_SLOTS + j + 1))
                    src = adastream[bass.ds(ADA_SLOTS * r + (ADA_FIRST + j), 1)].rearrange("a p n -> p (a n)")
                    pool.dma_start(ada[:, j, :], src).then_inc(ada_in[j], 16)
            if n_ada2:
                for j in range(ADA_SLOTS):
                    pool.wait_ge(ada_done, 2 * ADA1 - ADA_SLOTS + j + 1)
                    pool.dma_start(ada[:, j, :], adastream[2 * ADA1 + j]).then_inc(ada_in[j], 16)
                pool.dma_start(cond[:, :, :], c_rows[:, 1:3, :]).then_inc(cond2_in, 16)
                with nc.gpsimd.Fori(1, n_ada2) as r:
                    for j in range(ADA_SLOTS):
                        pool.wait_ge(ada_done, 2 * ADA_SLOTS * r + (2 * ADA1 - 2 * ADA_SLOTS + 2 * j + 2))
                        src = adastream[bass.ds(ADA_SLOTS * r + (2 * ADA1 + j), 1)].rearrange("a p n -> p (a n)")
                        pool.dma_start(ada[:, j, :], src).then_inc(ada_in[j], 16)

        @block.scalar
        def _(act):
            step = [0]

            def link(ins):
                step[0] += 1
                ins.then_inc(act_step, 1)
                act.wait_ge(act_step, step[0])

            def split_hi(q, dp=0, n=None):
                n = n or width(q)
                act.wait_ge(raw_in[q % SLOTS], 16 * (q // SLOTS + 1) + 16 // SLOTS * dp)
                if q >= SLOTS - 1:
                    act.wait_ge(panel_used, USED0 + q - SLOTS + 1 + dp)
                nc.scalar.activation(whi[:, q % SLOTS, 0:n], raw[:, q % SLOTS, 0:n], ACT.Copy).then_inc(hi_split, 1)

            def square(T, g, group, di=0):
                if g >= 2:
                    act.wait_ge(acc_done, 3 * group + g - 1 + 3 * di)
                dst = stage_a if g else stage_b
                nc.scalar.activation(dst[:, :, 0:T], X[:, 2 * g:2 * g + 2, 0:T], ACT.Square).then_inc(sq_done, 1)

            def squares(T, group):
                for g in range(KD // 2):
                    square(T, g, group)

            def roots(n):
                w = NORMS[n][0] // PART
                act.wait_ge(ms_ready, n + 1)
                nc.scalar.activation(root[:, 0:w], ms[:, 0:w], ACT.Sqrt).then_inc(root_ready, 1)

            def linear_out(name, T):
                for g in range(KD // 2):
                    for q in range(2 * g + AHEAD, 2 * g + AHEAD + 2):
                        split_hi(P0[name] + q)
                    act.wait_ge(evacuated, G0[name] + g + 1)
                    square(T, g, SET0[name])

            def modulate(n):
                T, amp, shift = NORMS[n]
                b = KD * modulated(n)
                for c in range(KD):
                    act.wait_ge(xhat_ready, b + c + 1)
                    if c >= 2:
                        act.wait_ge(h_ready, b + c - 1)
                    for dst in (stage_b[:, c % 2, :], h_hi[T][:, c, :]):
                        for lo, hi, s in halves(T):
                            ins = nc.scalar.activation(dst[:, lo:hi], stage_a[:, c % 2, lo:hi], ACT.Identity,
                                                       scale=amp(c, s), bias=shift(c, s))
                    ins.then_inc(h_hi_ready, 1)

            def linear_splits(name, n):
                with nc.scalar.Fori(0, n // 4) as i:
                    for j in range(4):
                        split_hi(P0[name] + j + AHEAD, 4 * i)

            def ffn(name):
                e0, n, T, _ = FFN[name]
                p0, g0 = P0[name], G0[name]
                full = PANEL * PART
                with nc.scalar.Fori(0, n) as i:
                    nxt = AHEAD
                    for u in range(UNITS):
                        while nxt <= 2 * KD * max(u + 1, 2) // PANEL + AHEAD:
                            split_hi(p0 + nxt, EXPERT_PANELS * i, full)
                            nxt += 1
                        if u == 0 and name in SET0:
                            act.wait_ge(acc_done, 3 * SET0[name] + 3 * i)
                        if u < UNITS - 1:
                            act.wait_ge(unit_done, (UNITS - 1) * (e0 + i) + u + 1)
                        else:
                            act.wait_ge(panel_used, USED0 + p0 + 2 * KD * UNITS // PANEL + EXPERT_PANELS * i)
                        nc.scalar.activation(stage_a[:, u % 2, 0:T], PS[:, 2 * (u % 3), 0:T],
                                             ACT.Silu).then_inc(silu_done, 1)
                        act.wait_ge(evacuated, g0 + u + 1 + EXPERT_GROUPS * i)
                        nc.scalar.activation(hid_hi[T][:, u, :], stage_b[:, u % 2, 0:T], ACT.Copy).then_inc(hid_hi_done, 1)
                    if name in SET0:
                        act.wait_ge(hid_ready, UNITS * (e0 + i) + UNITS)
                    for g in range(KD // 2):
                        while nxt <= 2 * KD * UNITS // PANEL + 2 * g + 1 + AHEAD:
                            split_hi(p0 + nxt, EXPERT_PANELS * i, full)
                            nxt += 1
                        if name in SET0:
                            act.wait_ge(evacuated, g0 + UNITS + g + 1 + EXPERT_GROUPS * i)
                            square(T, g, SET0[name], i)

            per = ADA_FIRST // 6
            act.dma_start(cond[:, 0, :], c_rows[:, 0, :]).then_inc(cond_in, 16)
            for j in range(6):
                src = adastream[per * j:per * j + per].rearrange("a p n -> p a n")
                act.dma_start(ada_first[:, per * j:per * j + per, :], src).then_inc(ada_first_in[j], 16)
            act.wait_ge(x_in, 16)
            squares(SEQ, 0)
            act.wait_ge(cond_in, 16)
            nc.scalar.activation(cond[:, 0, :], cond[:, 0, :], ACT.Silu).then_inc(cond_ready, 1)
            act.wait_ge(S("angle_reduced"), 1)
            nc.scalar.activation(trig[:, 1, :], red, ACT.Sin)
            nc.scalar.activation(turns, red, ACT.Abs).then_inc(S("angle_abs"), 1)
            act.wait_ge(S("angle_cos"), 1)
            nc.scalar.activation(trig[:, 0, :], angle, ACT.Sin).then_inc(S("trig_ready"), 1)
            for q in range(AHEAD):
                split_hi(q)

            def mixer(l):
                win, wout = f"win{l}", f"wout{l}"
                linear_splits(win, 28)
                act.wait_ge(S("z_ready"), l + 1)
                link(nc.scalar.activation(m["ln"], m["zb"], ACT.Abs))
                link(nc.scalar.activation(m["ln"], m["ln"], ACT.Exp, scale=-1.0))
                nc.scalar.activation(m["ln"], m["ln"], ACT.Ln, bias=1.0).then_inc(S("ln_ready"), 1)
                act.wait_ge(S("cum_ready"), l + 1)
                nc.scalar.activation(m["eb"], m["cum_a"], ACT.Exp)
                nc.scalar.activation(m["enb"], m["cum_a"], ACT.Exp, scale=-1.0)
                for f in range(2):
                    for c in range(SEQ // CHUNK):
                        e = CHUNK * (c + 1)
                        ins = nc.scalar.activation(m["ekd"][:, f, e - CHUNK:e], m["cum_a"][:, f, e - CHUNK:e], ACT.Exp,
                                                   scale=-1.0, bias=m["cum_a"][:, f, e - 1:e])
                ins.then_inc(S("exps_ready"), 1)
                act.wait_ge(evacuated, G0[win] + 10)
                nc.scalar.activation(m["prj"][:, 12:20, :], m["prj"][:, 12:20, :], ACT.Silu).then_inc(S("gates_ready"), 1)
                act.wait_ge(S("kd_turned"), l + 1)
                nc.scalar.activation(m["kdt"].rearrange("p a b -> p (a b)"), PS[:, 7, :], ACT.Copy).then_inc(S("kdt_ready"), 1)
                act.wait_ge(S("o_done"), l + 1)
                nc.scalar.activation(m["o"], PS[:, 0:4, :].rearrange("p b (h t) -> p (b h) t", h=2), ACT.Copy).then_inc(S("o_copied"), 1)
                act.wait_ge(S("o_centred"), l + 1)
                nc.scalar.activation(m["osq"], m["o"], ACT.Square).then_inc(S("osq_ready"), 1)
                act.wait_ge(S("oms_ready"), l + 1)
                nc.scalar.activation(root[:, 0:16], ms[:, 0:16], ACT.Sqrt).then_inc(S("oroot_ready"), 1)
                act.wait_ge(S("o_normed"), l + 1)
                for h in range(HEADS):
                    ins = nc.scalar.activation(m["o"][:, HEADS + h, :], m["o"][:, HEADS + h, :], ACT.Identity,
                                               scale=V("gn_g", HEADS * l + h), bias=V("gn_b", HEADS * l + h))
                ins.then_inc(S("o_affine"), 1)
                for half in range(2):
                    act.wait_ge(S("o_gated"), 2 * l + half + 1)
                    heads = slice(HEADS * half, HEADS * half + HEADS)
                    nc.scalar.activation(h_hi[SEQ][:, heads, :], m["o"][:, heads, :], ACT.Copy).then_inc(S("o_hi"), 1)
                linear_out(wout, SEQ)

            for l, ff in enumerate(("dense", "moe")):
                if runs(f"win{l}"):
                    roots(2 * l)
                    modulate(2 * l)
                    mixer(l)
                if runs(ff):
                    roots(2 * l + 1)
                    modulate(2 * l + 1)
                    if ff == "moe":
                        act.wait_ge(cond2_in, 16)
                        nc.scalar.activation(cond[:, :, :], cond[:, :, :], ACT.Silu).then_inc(cond_ready, 1)
                        for t in range(2):
                            act.wait_ge(S("gap_ready"), t + 1)
                            nc.scalar.activation(gt[:, t, 25:26], gt[:, t, 24:25], ACT.Exp).then_inc(S("gap_exp"), 1)
                    ffn(ff)
            if runs("ffn00"):
                roots(FINAL1)
                act.wait_ge(S("block1_out"), 1)
                act.wait_ge(ctx_in, 16)
                squares(BOTH, NORM_SET[5])
                roots(5)
                modulate(5)
                ffn("ffn00")
            if runs("conv_cu"):
                roots(6)
                modulate(6)
                for f in range(KD):
                    q = P0["conv_cu"] + 2 * f
                    split_hi(q + AHEAD)
                    split_hi(q + AHEAD + 1)
                    act.wait_ge(panel_used, USED0 + max(q + 2, P0["conv_cu"] + 4))
                    if f >= 2:
                        act.wait_ge(evacuated, G0["conv_cu"] + f - 1)
                    nc.scalar.activation(stage_a[:, f % 2, :], PS[:, 2 * (f % 2), :], ACT.Copy).then_inc(S("conv_c"), 1)
                for f in range(KD):
                    split_hi(P0["conv_b"] + f + AHEAD)
                    if f % 2:
                        for k in (f - 1, f):
                            act.wait_ge(S("y_ready"), k + 1)
                            nc.scalar.activation(y_hi[:, k, :], stage_b[:, k % 2, :], ACT.Copy).then_inc(S("y_hi"), 1)
                linear_out("conv_out", BOTH)
            if runs("ffn01"):
                roots(7)
                modulate(7)
                ffn("ffn01")
            if runs("ffn10"):
                roots(8)
                modulate(8)
                ffn("ffn10")
            if runs("mla"):
                roots(9)
                modulate(9)
                p0, g0 = P0["mla"], G0["mla"]
                for q in range(4):
                    split_hi(p0 + q + AHEAD)
                act.wait_ge(evacuated, g0 + 2)
                nc.scalar.activation(late[:, 0:1024], stage_a[:, :, :].rearrange("p a b -> p (a b)"),
                                     ACT.Square).then_inc(S("lat_sq"), 1)
                act.wait_ge(S("lat_ms"), 1)
                nc.scalar.activation(root[:, 0:6], ms[:, 0:6], ACT.Sqrt).then_inc(S("lat_root"), 1)
                act.wait_ge(S("lat_normed"), 1)
                nc.scalar.activation(cq_hi[:, :, :].rearrange("p a b -> p (a b)"), late[:, 0:512], ACT.Copy)
                nc.scalar.activation(ckv_hi[:, :], late[:, 512:1024], ACT.Copy).then_inc(S("lat_hi"), 1)
                for q in range(4, 9):
                    split_hi(p0 + q + AHEAD)
                def qk_square(r):
                    act.wait_ge(evacuated, g0 + (5, 7, 9)[r])
                    if r:
                        act.wait_ge(S("qk_sum"), r)
                    src = X[:, :, SEQ:BOTH] if r == 0 else kn[:, 4 * r - 4:4 * r, :]
                    dst = late[:, 0:2048].rearrange("p (h t) -> p h t", h=src.shape[1])
                    nc.scalar.activation(dst, src, ACT.Square).then_inc(S("qk_sq"), 1)

                def qk_roots(r):
                    act.wait_ge(S("qk_ms"), r + 1)
                    c = slice(16 * (r % 2), 16 * (r % 2) + 16)
                    nc.scalar.activation(root[:, c], ms[:, c], ACT.Sqrt).then_inc(S("qk_root"), 1)

                act.wait_ge(evacuated, g0 + 5)
                nc.scalar.activation(stage_a[:, :, :].rearrange("p a b -> p (a b)"), qr[:, :, :].rearrange("p a b -> p (a b)"), ACT.Square)
                nc.scalar.activation(stage_b[:, 1, :], stage_b[:, 0, :], ACT.Square)
                qk_square(0)
                qk_square(1)
                qk_roots(0)
                qk_square(2)
                qk_roots(1)
                qk_roots(2)

                def head_part(h):
                    act.wait_ge(S("head_done"), h + 1)
                    nc.scalar.activation(h_hi[SEQ][:, h, :], PS[:, 4 + h % 2, 0:SEQ], ACT.Copy).then_inc(S("head_hi"), 1)

                for h in range(MLA_HEADS + 2):
                    if h < MLA_HEADS:
                        for t in range(2):
                            act.wait_ge(S("neg_max"), 2 * h + t + 1)
                            if h >= 2:
                                act.wait_ge(S("p_turned"), 2 * h + t - 3)
                            c = 2 * (h % 2) + t
                            nc.scalar.activation(probs[:, h % 2, t, :], PS[:, SCORE_BANK[h % 2] + t, :], ACT.Exp, bias=ms[:, c:c + 1],
                                                 accum_out=root[:, c:c + 1]).then_inc(S("exp_done"), 1)
                    if 0 < h <= MLA_HEADS:
                        if h >= 3:
                            act.wait_ge(S("head_done"), h - 2)
                        for t in range(2):
                            act.wait_ge(S("p_turned"), 2 * h + t - 1)
                            nc.scalar.activation(pts[:, (h - 1) % 2, :, PART * t:PART * t + PART],
                                                 PS[:, 2 + t, :].rearrange("p (k q) -> p k q", k=4), ACT.Copy).then_inc(S("pt_copied"), 1)
                    if h >= 2:
                        head_part(h - 2)
            if runs("mla_o"):
                linear_out("mla_o", SEQ)
            if runs("ffn11"):
                roots(10)
                modulate(10)
                ffn("ffn11")

        @block.vector
        def _(dve):
            step = [0]

            def link(ins):
                step[0] += 1
                ins.then_inc(dve_step, 1)
                dve.wait_ge(dve_step, step[0])

            def split_lo(q, dp=0, n=None):
                n = n or width(q)
                dve.wait_ge(hi_split, q + 1 + dp)
                if q >= SLOTS - 1:
                    dve.wait_ge(panel_used, USED0 + q - SLOTS + 1 + dp)
                nc.vector.tensor_tensor(wlo[:, q % SLOTS, 0:n], raw[:, q % SLOTS, 0:n], whi[:, q % SLOTS, 0:n].bitcast(F32),
                                        ALU.subtract).then_inc(lo_split, 1)

            def spread(dst, cols, n):
                return nc.vector.tensor_tensor(dst, ident.unsqueeze(1).broadcast_to([PART, n, PART]),
                                               cols.unsqueeze(2).broadcast_to([PART, n, PART]), ALU.mult)

            def add_squares(T, g, group, di=0):
                dve.wait_ge(sq_done, 4 * group + g + 1 + 4 * di)
                if g > 1:
                    dve.wait_ge(acc_done, 3 * group + g - 1 + 3 * di)
                nc.vector.tensor_tensor(stage_b[:, :, 0:T], stage_b[:, :, 0:T], stage_a[:, :, 0:T], ALU.add).then_inc(acc_done, 1)

            def modulation(t, weights, cols, first, di=0, bank=6):
                waste = PS[:, bank:bank + 2, :].rearrange("p a b -> p (a b)")
                for k, col in enumerate(cols):
                    if first + k:
                        dve.wait_ge(ada_done, first + k + di)
                    nc.vector.scalar_tensor_tensor(out=waste, in0=weights, scalar=1.0, in1=cond[:, k, :], op0=ALU.mult, op1=ALU.mult,
                                                   accum_out=col).then_inc(ada_done, 1)

            def ring_tile(t, cols, first, rounds_on=0, di=0):
                r = t - ADA_FIRST
                dve.wait_ge(ada_in[r % ADA_SLOTS], 16 * (r // ADA_SLOTS + 1) + rounds_on)
                modulation(t, ada[:, r % ADA_SLOTS, :], cols, first, di)

            def norm(n):
                T = NORMS[n][0]
                w = T // PART
                dve.wait_ge(sumsq_ready, n + 1)
                nc.vector.tensor_scalar(ms[:, 0:w], PS[:, BC_BANK, SUMS:SUMS + w], 1.0 / D, EPS,
                                        ALU.mult, ALU.add).then_inc(ms_ready, 1)
                dve.wait_ge(root_ready, n + 1)
                link(nc.vector.reciprocal(rstd[:, 0:w], root[:, 0:w]))
                spread(diag[:, 0:w, :], rstd[:, 0:w], w).then_inc(diag_ready, 1)
                dve.wait_ge(bc_ready, n + 1)
                if n == FINAL1:
                    for c in range(KD):
                        ins = nc.vector.scalar_tensor_tensor(out=X[:, c, 0:T], in0=X[:, c, 0:T], scalar=V("final_g", c),
                                                             in1=PS[:, BC_BANK, 0:T], op0=ALU.mult, op1=ALU.mult)
                    ins.then_inc(S("block1_out"), 1)
                    return
                b = KD * modulated(n)
                for c in range(KD + 1):
                    if c < KD:
                        nc.vector.tensor_tensor(stage_a[:, c % 2, 0:T], X[:, c, 0:T], PS[:, BC_BANK, 0:T],
                                                ALU.mult).then_inc(xhat_ready, 1)
                    if c:
                        dve.wait_ge(h_hi_ready, b + c)
                        nc.vector.tensor_tensor(h_lo[T][:, c - 1, :], stage_b[:, (c - 1) % 2, 0:T],
                                                h_hi[T][:, c - 1, :].bitcast(F32), ALU.subtract).then_inc(h_ready, 1)

            def mods1(l, which, lo, hi):
                dve.wait_ge(ada_done, ADA1 * l + hi)
                link(nc.vector.tensor_tensor(mod1[:, l, lo:hi], mod1[:, l, lo:hi], V("ada_b", ADA1 * l + lo, hi - lo), ALU.add))
                for w in which:
                    ins = nc.vector.scalar_tensor_tensor(out=amp1[:, l, w, :], in0=mod1[:, l, 24 * w + 8:24 * w + 16], scalar=1.0,
                                                         in1=V(("mix_g", "ffn_g")[w], KD * l, KD), op0=ALU.add, op1=ALU.mult)
                link(ins)

            def mods2(l, parts):
                lo, hi = 24 * parts[0], 24 * parts[-1] + 24
                dve.wait_ge(ada_done, 2 * ADA1 + 2 * ADA2 * l + 2 * hi)
                link(nc.vector.tensor_tensor(mod2[:, l, lo:hi, :], mod2[:, l, lo:hi, :],
                                             V("mod_b", 72 * l + lo, hi - lo).unsqueeze(2).broadcast_to([PART, hi - lo, 2]), ALU.add))
                for w in parts:
                    nc.vector.scalar_tensor_tensor(out=amp2[:, l, w, :, :], in0=mod2[:, l, 24 * w + 8:24 * w + 16, :], scalar=1.0,
                                                   in1=V("g2", 24 * l + 8 * w, KD).unsqueeze(2).broadcast_to([PART, KD, 2]),
                                                   op0=ALU.add, op1=ALU.mult)
                    ins = nc.vector.tensor_scalar(gate2[:, l, w, :, :], mod2[:, l, 24 * w + 16:24 * w + 24, :],
                                                  1.0 if w == 1 else 0.5, None, ALU.mult)
                link(ins)

            def add_tile(t, pair, k, T, gate):
                for lo, hi, s in halves(T):
                    ins = nc.vector.scalar_tensor_tensor(out=X[:, t, lo:hi], in0=PS[:, 2 * pair + k, lo:hi], scalar=gate(t, s),
                                                         in1=X[:, t, lo:hi], op0=ALU.mult, op1=ALU.add)
                return ins

            def linear_out(name, T, gate):
                for g in range(4):
                    split_lo(P0[name] + 2 * g + AHEAD)
                    split_lo(P0[name] + 2 * g + AHEAD + 1)
                    dve.wait_ge(panel_used, USED0 + P0[name] + 2 * g + 2)
                    for k in range(2):
                        ins = add_tile(2 * g + k, g % 2, k, T, gate)
                    ins.then_inc(evacuated, 1)
                    if g >= 2:
                        add_squares(T, g - 1, SET0[name])
                add_squares(T, KD // 2 - 1, SET0[name])

            def ffn(name, gate):
                e0, n, T, beside = FFN[name]
                p0 = P0[name]
                full = PANEL * PART

                def splits(first, last, i):
                    for q in range(first, last + 1):
                        split_lo(p0 + q, EXPERT_PANELS * i, full)

                def beside_tile(done, i):
                    t, per = beside[0] + done, beside[1]
                    if name == "dense":
                        ring_tile(t, [mod1[:, 1, bass.ds(per * i + done, 1)]], t, 16 * (per // ADA_SLOTS) * i, per * i)
                    else:
                        l, at = divmod(t - 2 * ADA1, ADA2)
                        ring_tile(t, [mod2[:, l, bass.ds(per * i + at, 1), k] for k in range(2)],
                                  2 * t - 2 * ADA1, 16 * (per // ADA_SLOTS) * i, 2 * per * i)

                with nc.vector.Fori(0, n) as i:
                    nxt, done = AHEAD, 0
                    for u in range(UNITS):
                        if u == 0:
                            splits(nxt, 4 * KD // PANEL + AHEAD, i)
                            nxt = 4 * KD // PANEL + AHEAD + 1
                        if u == 0 and name in SET0:
                            dve.wait_ge(acc_done, 3 * SET0[name] + 3 * i)
                        dve.wait_ge(silu_done, UNITS * (e0 + i) + u + 1)
                        nc.vector.tensor_tensor(stage_b[:, u % 2, 0:T], stage_a[:, u % 2, 0:T], PS[:, 2 * (u % 3) + 1, 0:T],
                                                ALU.mult).then_inc(evacuated, 1)
                        dve.wait_ge(hid_hi_done, UNITS * (e0 + i) + u + 1)
                        nc.vector.tensor_tensor(hid_lo[T][:, u, :], stage_b[:, u % 2, 0:T], hid_hi[T][:, u, :].bitcast(F32),
                                                ALU.subtract).then_inc(hid_ready, 1)
                        if u:
                            splits(nxt, 2 * KD * (u + 1) // PANEL + AHEAD, i)
                            nxt = max(nxt, 2 * KD * (u + 1) // PANEL + AHEAD + 1)
                        while beside and done < beside[1] * 5 * (u + 1) // (6 * UNITS):
                            beside_tile(done, i)
                            done += 1
                    for g in range(KD // 2):
                        first = 2 * KD * UNITS // PANEL + 2 * g
                        splits(nxt, first + 1 + AHEAD, i)
                        nxt = first + 2 + AHEAD
                        dve.wait_ge(panel_used, USED0 + p0 + first + 2 + EXPERT_PANELS * i)
                        pair = (UNITS + g) % 3
                        if name == "moe":
                            dve.wait_ge(evacuated, G0[name] + UNITS + g + EXPERT_GROUPS * i)
                            ge = gates[:, bass.ds(i, 1), :].broadcast_to([PART, 2, SEQ])
                            nc.vector.tensor_tensor(gated[:, :, :], PS[:, 2 * pair:2 * pair + 2, 0:SEQ], ge,
                                                    ALU.mult).then_inc(S("gated_done"), 1)
                            dve.wait_ge(S("gated_done"), 4 * i + g + 1)
                            for k in range(2):
                                t = 2 * g + k
                                ins = nc.vector.scalar_tensor_tensor(out=X[:, t, 0:SEQ], in0=gated[:, k, :], scalar=gate(t, 0),
                                                                     in1=X[:, t, 0:SEQ], op0=ALU.mult, op1=ALU.add)
                        else:
                            for k in range(2):
                                ins = add_tile(2 * g + k, pair, k, T, gate)
                        ins.then_inc(evacuated, 1)
                        if g >= 2 and name in SET0:
                            add_squares(T, g - 1, SET0[name], i)
                        while beside and done < beside[1] and g < KD // 2 - 1:
                            beside_tile(done, i)
                            done += 1
                            if done % 2 == 0:
                                break
                    if name in SET0:
                        add_squares(T, KD // 2 - 1, SET0[name], i)

            def angles():
                link(nc.vector.tensor_copy(angle, posi.bitcast(I32)))
                link(nc.vector.tensor_scalar(angle, angle, C("inv_freq"), None, ALU.mult))
                link(nc.vector.tensor_scalar(turns, angle, 1.0 / TWO_PI, ROUND, ALU.mult, ALU.add))
                link(nc.vector.tensor_scalar(turns, turns, ROUND, None, ALU.subtract))
                link(nc.vector.scalar_tensor_tensor(out=red, in0=turns, scalar=-PI_HI, in1=angle, op0=ALU.mult, op1=ALU.add))
                link(nc.vector.scalar_tensor_tensor(out=red, in0=turns, scalar=-PI_MID, in1=red, op0=ALU.mult, op1=ALU.add))
                link(nc.vector.scalar_tensor_tensor(out=red, in0=turns, scalar=-PI_LO, in1=red, op0=ALU.mult, op1=ALU.add))
                nc.vector.tensor_scalar(red, red, PI_MAX, -PI_MAX, ALU.min, ALU.max).then_inc(S("angle_reduced"), 1)
                dve.wait_ge(S("angle_abs"), 1)
                nc.vector.tensor_scalar(angle, turns, -1.0, float(np.pi / 2), ALU.mult, ALU.add).then_inc(S("angle_cos"), 1)

            def mixer(l):
                win, wout = f"win{l}", f"wout{l}"
                prj, val, o = m["prj"], m["val"], m["o"]
                for g in range(12):
                    first, end = (2 * g, 2 * g + 2) if g < 10 else (4 * g - 20, 4 * g - 16)
                    if g == 10:
                        dve.wait_ge(S("ga_done"), l + 1)
                        nc.vector.tensor_copy(m["ga"], PS[0:RANK, 4, 0:SEQ]).then_inc(S("ga_copied"), 1)
                    if g == 11:
                        dve.wait_ge(S("z_done"), l + 1)
                        for f in range(2):
                            ins = nc.vector.tensor_scalar(m["zb"][:, f, :], PS[:, 7, SEQ * f:SEQ * f + SEQ], V("alpha_b", 2 * l + f), None, ALU.add)
                        ins.then_inc(S("z_ready"), 1)
                    for q in range(first, end):
                        split_lo(P0[win] + q + AHEAD)
                    dve.wait_ge(panel_used, USED0 + P0[win] + max(end, 4))
                    dst, n = (prj[:, 2 * g:2 * g + 2, :], SEQ) if g < 10 else (val[:, :, 512 * (g - 10):512 * (g - 9)], 512)
                    nc.vector.tensor_copy(dst, PS[:, 2 * (g % 2):2 * (g % 2) + 2, 0:n]).then_inc(evacuated, 1)
                    done, per = ((ADA_FIRST, 3), (30, 2))[l]
                    for t in range(done + per * g, min(done + per * g + per, ADA1)):
                        ring_tile(ADA1 * l + t, [mod1[:, l, t:t + 1]], ADA1 * l + t)
                if l == 0:
                    mods1(0, (1,), 2 * KD, ADA1)
                else:
                    mods1(1, (1,), 30, ADA1)
                dve.wait_ge(S("ln_ready"), l + 1)
                link(nc.vector.scalar_tensor_tensor(out=m["cum_a"], in0=m["zb"], scalar=0.0, in1=m["ln"], op0=ALU.min, op1=ALU.subtract))
                src, dst = m["cum_a"].rearrange("p f (c t) -> p (f c) t", t=CHUNK), m["cum_b"].rearrange("p f (c t) -> p (f c) t", t=CHUNK)
                link(nc.vector.tensor_scalar(m["cum_a"], m["cum_a"], 1.0 / GLA_TAU, None, ALU.mult))
                d = 1
                while d < CHUNK:
                    nc.vector.tensor_copy(dst[:, :, 0:d], src[:, :, 0:d])
                    ins = nc.vector.tensor_tensor(dst[:, :, d:CHUNK], src[:, :, d:CHUNK], src[:, :, 0:CHUNK - d], ALU.add)
                    src, dst, d = dst, src, 2 * d
                    if d < CHUNK:
                        link(ins)
                ins.then_inc(S("cum_ready"), 1)
                dve.wait_ge(S("turned"), l + 1)
                cos = trig[:, 0, :].unsqueeze(1).broadcast_to([PART, HEADS, SEQ])
                sin = trig[:, 1, :].unsqueeze(1).broadcast_to([PART, HEADS, SEQ])
                for k in range(2):
                    x = prj[:, 4 + 4 * k:8 + 4 * k, :]
                    nc.vector.tensor_tensor(m["t1"], x, cos, ALU.mult)
                    link(nc.vector.tensor_tensor(m["t2"], sin, PS[:, 2 * k:2 * k + 2, :].rearrange("p b (h t) -> p (b h) t", h=2), ALU.mult))
                    ins = nc.vector.tensor_tensor(x, m["t1"], m["t2"], ALU.add)
                    if k == 0:
                        link(ins)
                ins.then_inc(S("rotated"), 1)
                dve.wait_ge(S("exps_ready"), l + 1)
                q, k = prj[:, 0:2, :], prj[:, 2:4, :]
                nc.vector.scalar_tensor_tensor(out=m["qb"], in0=q, scalar=GLA_DK ** -0.5, in1=m["enb"], op0=ALU.mult, op1=ALU.mult)
                nc.vector.scalar_tensor_tensor(out=q, in0=q, scalar=GLA_DK ** -0.5, in1=m["eb"], op0=ALU.mult, op1=ALU.mult)
                nc.vector.tensor_tensor(m["kb"], k, m["eb"], ALU.mult)
                nc.vector.tensor_tensor(m["kd"], k, m["ekd"], ALU.mult)
                nc.vector.tensor_tensor(k, k, m["enb"], ALU.mult).then_inc(S("gla_qk"), 1)
                dve.wait_ge(S("ret_scores"), l + 1)
                dec = C("ret_decay")
                for j in range(2):
                    ins = nc.vector.tensor_tensor(m["sr"][:, j, :], dec, PS[:, 4 + j, :], ALU.mult)
                ins.then_inc(S("sr_ready"), 1)
                dve.wait_ge(S("ret_kt"), l + 1)
                rk = C("ret_k").unsqueeze(2).broadcast_to([PART, HEADS, PART])
                for j in range(2):
                    ins = nc.vector.tensor_tensor(m["kdr"][:, j, :].rearrange("p (h d) -> p h d", h=HEADS), rk,
                                                  PS[:, j, :].rearrange("p (h d) -> p h d", h=HEADS), ALU.mult)
                ins.then_inc(S("kdr_ready"), 1)
                for h in range(HEADS):
                    x = prj[:, 4 + h, :].rearrange("p (c t) -> p c t", t=CHUNK)
                    ins = nc.vector.tensor_tensor(x, x, C("ret_q")[:, CHUNK * h:CHUNK * h + CHUNK].unsqueeze(1).broadcast_to(
                        [PART, SEQ // CHUNK, CHUNK]), ALU.mult)
                ins.then_inc(S("qd_ready"), 1)
                nc.vector.memset(m["gs"], 0.0)
                nc.vector.memset(m["sc"], 0.0).then_inc(S("sc_zero"), 1)
                dve.wait_ge(S("sc_zero"), l + 1)
                dve.wait_ge(S("gla_scores"), l + 1)
                for way, name in enumerate(("causal", "anti")):
                    mask = C(name).bitcast(U32).unsqueeze(1).broadcast_to([PART, 2, PART])
                    for j in range(2):
                        heads = m["sc"][:, j, :].rearrange("p (a b t) -> p a b t", a=2, b=2)
                        for half in range(2):
                            ins = nc.vector.copy_predicated(heads[:, :, half, :], mask,
                                                            PS[:, 2 + 2 * j + half, 256 * way:256 * way + 256].rearrange("p (h t) -> p h t", h=2))
                    if way == 0:
                        link(ins)
                ins.then_inc(S("sc_ready"), 1)
                gs, rs = m["gs"], m["rs"]
                dve.wait_ge(S("gla_upd"), l + 1)
                for c, bank in enumerate((0, 1, 7)):
                    for f in range(2):
                        for hh in range(2):
                            r = slice(64 * hh, 64 * hh + 64)
                            upd = PS[r, bank, 256 * f + PART * hh:256 * f + PART * hh + PART]
                            h = 2 * f + hh
                            if c == 0:
                                ins = nc.vector.tensor_copy(gs[r, 0, h, :], upd)
                            else:
                                ins = nc.vector.scalar_tensor_tensor(
                                    out=gs[r, c, h, :], in0=gs[r, c - 1, h, :], scalar=m["eb"][r, f, CHUNK * c + CHUNK - 1:CHUNK * c + CHUNK],
                                    in1=upd, op0=ALU.mult, op1=ALU.add)
                    if c < 2:
                        link(ins)
                ins.then_inc(S("gs_ready"), 1)
                dve.wait_ge(S("ret_upd"), l + 1)
                for c, bank in enumerate((2, 3, 4)):
                    if c == 0:
                        link(nc.vector.tensor_copy(rs[:, 0, :], PS[:, bank, :]))
                        continue
                    for h in range(HEADS):
                        w = slice(PART * h, PART * h + PART)
                        ins = nc.vector.scalar_tensor_tensor(out=rs[:, c, w], in0=rs[:, c - 1, w], scalar=float(gammas()[h] ** CHUNK),
                                                             in1=PS[:, bank, w], op0=ALU.mult, op1=ALU.add)
                    if c < 2:
                        link(ins)
                ins.then_inc(S("rs_ready"), 1)
                dve.wait_ge(S("mean_done"), l + 1)
                ret = o[:, HEADS:2 * HEADS, :]
                nc.vector.scalar_tensor_tensor(out=ret, in0=PS[:, 4:6, :].rearrange("p b (h t) -> p (b h) t", h=2), scalar=-1.0 / RET_DK,
                                               in1=ret, op0=ALU.mult, op1=ALU.add).then_inc(S("o_centred"), 1)
                dve.wait_ge(S("o_sums"), l + 1)
                nc.vector.tensor_scalar(ms[:, 0:16], PS[:, 7, 0:16], 1.0 / RET_DK, EPS, ALU.mult, ALU.add).then_inc(S("oms_ready"), 1)
                dve.wait_ge(S("oroot_ready"), l + 1)
                link(nc.vector.reciprocal(rstd[:, 0:16], root[:, 0:16]))
                spread(m["odiag"], rstd[:, 0:16], 16).then_inc(S("odiag_ready"), 1)
                dve.wait_ge(S("o_spread"), l + 1)
                nc.vector.tensor_tensor(o, o, PS[:, 0:4, :].rearrange("p b (h t) -> p (b h) t", h=2), ALU.mult).then_inc(S("o_normed"), 1)
                dve.wait_ge(S("o_normed"), l + 1)
                dve.wait_ge(S("gates_ready"), l + 1)
                for h in range(HEADS):
                    ins = nc.vector.scalar_tensor_tensor(out=o[:, h, :], in0=o[:, h, :], scalar=V("gla_g", HEADS * l + h),
                                                         in1=prj[:, 12 + h, :], op0=ALU.mult, op1=ALU.mult)
                ins.then_inc(S("o_gated"), 1)
                dve.wait_ge(S("o_affine"), l + 1)
                nc.vector.tensor_tensor(ret, ret, prj[:, 16:20, :], ALU.mult).then_inc(S("o_gated"), 1)
                for half in range(2):
                    dve.wait_ge(S("o_hi"), 2 * l + half + 1)
                    heads = slice(HEADS * half, HEADS * half + HEADS)
                    ins = nc.vector.tensor_tensor(h_lo[SEQ][:, heads, :], o[:, heads, :], h_hi[SEQ][:, heads, :].bitcast(F32), ALU.subtract)
                ins.then_inc(S("o_ready"), 1)
                linear_out(wout, SEQ, lambda t, s: mod1[:, l, 16 + t:17 + t])

            def route():
                for t in range(2):
                    g = gt[:, t, :]
                    dve.wait_ge(S("logits"), 1)
                    link(nc.vector.tensor_copy(g[:, 0:8], PS[:, 5 + t, 0:8]))
                    link(nc.vector.max(g[:, 8:16], g[:, 0:8]))
                    link(nc.vector.max_index(gi[:, t, :], g[:, 8:16], g[:, 0:8]))
                    nc.vector.tensor_copy(g[:, 16:24], gi[:, t, :])
                    nc.vector.tensor_tensor(g[:, 24:25], g[:, 9:10], g[:, 8:9], ALU.subtract).then_inc(S("gap_ready"), 1)
                    dve.wait_ge(S("gap_exp"), t + 1)
                    link(nc.vector.tensor_scalar(g[:, 26:27], g[:, 25:26], 1.0, None, ALU.add))
                    link(nc.vector.reciprocal(g[:, 27:28], g[:, 26:27]))
                    link(nc.vector.tensor_tensor(g[:, 28:29], g[:, 25:26], g[:, 27:28], ALU.mult))
                    nc.vector.tensor_scalar(g[:, 32:40], C("iota"), g[:, 16:17], g[:, 27:28], ALU.is_equal, ALU.mult)
                    link(nc.vector.tensor_scalar(g[:, 40:48], C("iota"), g[:, 17:18], g[:, 28:29], ALU.is_equal, ALU.mult))
                    link(nc.vector.tensor_tensor(g[:, 48:56], g[:, 32:40], g[:, 40:48], ALU.add))
                    spread(gdiag[:, t, :, :], g[:, 48:56], N_EXPERTS).then_inc(S("gdiag_ready"), 1)
                for t in range(2):
                    dve.wait_ge(S("gates_spread"), t + 1)
                    ins = nc.vector.tensor_copy(gates[:, :, PART * t:PART * t + PART],
                                                PS[:, 2 * t:2 * t + 2, :].rearrange("p b (e t) -> p (b e) t", e=4))
                ins.then_inc(S("gates_in"), 1)

            def latent():
                p0, g0 = P0["mla"], G0["mla"]
                qn = X[:, :, SEQ:BOTH]
                nxt = AHEAD
                places = [(3, stage_a[:, 0, :].rearrange("p (f t) -> p f t", f=2), lambda b: b[:, :, 0:SEQ]),
                          (3, None, None),
                          (4, qn[:, 0:4, :], None), (5, qn[:, 4:8, :], None), (6, qr[:, :, :], None)]
                places += [(7, kn[:, 2 * i:2 * i + 2, :], lambda b: b) for i in range(4)]
                places += [(8, val2[:, i, :].rearrange("p (b n) -> p b n", b=2), lambda b: b) for i in range(4)]
                done = 0
                for g, (panel, dst, view) in enumerate(places):
                    while nxt <= panel + AHEAD:
                        split_lo(p0 + nxt)
                        nxt += 1
                    if g in (5, 6, 7, 9, 10, 11):
                        done += 1
                        dve.wait_ge(group_done, done)
                    else:
                        dve.wait_ge(panel_used, USED0 + p0 + panel + 1)
                    bank = PS[:, 2 * (g % 3):2 * (g % 3) + 2, :]
                    if g == 1:
                        nc.vector.tensor_copy(stage_a[:, 1, :], bank[:, 0, :])
                        ins = nc.vector.tensor_copy(stage_b[:, 0, :], bank[:, 1, :])
                    else:
                        src = view(bank) if view else bank.rearrange("p b (h t) -> p (b h) t", h=2)
                        ins = nc.vector.tensor_copy(dst, src)
                    ins.then_inc(evacuated, 1)
                    if g != 1:
                        continue
                    dve.wait_ge(S("lat_sum"), 1)
                    nc.vector.tensor_scalar(ms[:, 0:2], PS[:, BC_BANK, SUMS:SUMS + 2], 1.0 / Q_LORA, EPS, ALU.mult, ALU.add)
                    nc.vector.tensor_scalar(ms[:, 2:6], PS[:, BC_BANK, SUMS + 2:SUMS + 6], 1.0 / PART, EPS,
                                            ALU.mult, ALU.add).then_inc(S("lat_ms"), 1)
                    dve.wait_ge(S("lat_root"), 1)
                    link(nc.vector.reciprocal(rstd[:, 0:6], root[:, 0:6]))
                    spread(late[:, 1024:1792].rearrange("p (i t) -> p i t", i=6), rstd[:, 0:6], 6).then_inc(S("lat_diag"), 1)
                    dve.wait_ge(S("lat_bc"), 1)
                    for f in range(2):
                        nc.vector.scalar_tensor_tensor(out=late[:, SEQ * f:SEQ * f + SEQ], in0=stage_a[:, 0, SEQ * f:SEQ * f + SEQ],
                                                       scalar=V("qa_g", f), in1=PS[:, 4, 0:SEQ], op0=ALU.mult, op1=ALU.mult)
                    nc.vector.scalar_tensor_tensor(out=late[:, 512:1024], in0=stage_a[:, 1, :], scalar=V("kva_g", 0),
                                                   in1=PS[:, 5, :], op0=ALU.mult, op1=ALU.mult).then_inc(S("lat_normed"), 1)
                    dve.wait_ge(S("lat_hi"), 1)
                    nc.vector.tensor_tensor(cq_lo[:, :, :].rearrange("p a b -> p (a b)"), late[:, 0:512],
                                            cq_hi[:, :, :].rearrange("p a b -> p (a b)").bitcast(F32), ALU.subtract)
                    nc.vector.tensor_tensor(ckv_lo[:, :], late[:, 512:1024], ckv_hi[:, :].bitcast(F32), ALU.subtract).then_inc(S("lat_ready"), 1)
                low, high = slice(0, 64), slice(64, PART)
                def qk_inverse(r):
                    dve.wait_ge(S("qk_sum"), r + 1)
                    c = slice(16 * (r % 2), 16 * (r % 2) + 16)
                    if r == 0:
                        nc.vector.tensor_scalar(ms[:, 32:36], PS[:, 7, 32:36], 1.0 / QK_HEAD, EPS, ALU.mult, ALU.add)
                        nc.vector.tensor_scalar(ms[:, c], PS[:, 7, 0:16], 1.0 / QK_HEAD, EPS, ALU.mult, ALU.add).then_inc(S("qk_ms"), 1)
                    else:
                        nc.vector.scalar_tensor_tensor(out=ms[:, c].rearrange("p (h t) -> p h t", h=4), scalar=1.0 / QK_HEAD,
                                                       in0=PS[:, 5 + r, 16:32].rearrange("p (h t) -> p h t", h=4),
                                                       in1=ms[:, 32:36].unsqueeze(1).broadcast_to([PART, 4, 4]),
                                                       op0=ALU.mult, op1=ALU.add).then_inc(S("qk_ms"), 1)
                    dve.wait_ge(S("qk_root"), r + 1)
                    link(nc.vector.reciprocal(rstd[:, c], root[:, c]))
                    if r == 0:
                        link(nc.vector.tensor_scalar(rstd[:, c], rstd[:, c], QK_SCALE, None, ALU.mult))

                def qk_spread(r):
                    c = slice(16 * (r % 2), 16 * (r % 2) + 16)
                    spread(late[:, 2048:4096].rearrange("p (i t) -> p i t", i=16), rstd[:, c], 16).then_inc(S("qk_diag"), 1)

                def qk_norm(r):
                    dve.wait_ge(S("qk_bc"), r + 1)
                    if r == 0:
                        nc.vector.scalar_tensor_tensor(out=qn, in0=qn, scalar=V("q_g", 0),
                                                       in1=PS[:, 0:4, :].rearrange("p b (h t) -> p (b h) t", h=2), op0=ALU.mult, op1=ALU.mult)
                        for k, rows in enumerate((low, high)):
                            ins = nc.vector.scalar_tensor_tensor(out=qr[rows, :, :], in0=qr[rows, :, :], scalar=V("q_g", 1)[rows, :],
                                                                 in1=PS[rows, 0:4, SEQ * k:SEQ * k + SEQ], op0=ALU.mult, op1=ALU.mult)
                    else:
                        k0 = 4 * (r - 1)
                        nc.vector.scalar_tensor_tensor(out=kn[:, k0:k0 + 4, :], in0=kn[:, k0:k0 + 4, :], scalar=V("k_g", 0),
                                                       in1=PS[:, 0:4, :], op0=ALU.mult, op1=ALU.mult)
                        for i in range(2):
                            for k, rows in enumerate((low, high)):
                                ins = nc.vector.scalar_tensor_tensor(out=krt[rows, k0 // 2 + i, :], in0=stage_b[rows, 0, :],
                                                                     scalar=V("k_g", 1)[rows, :], in1=PS[rows, 2 * i + k, :],
                                                                     op0=ALU.mult, op1=ALU.mult)
                    ins.then_inc(S("qk_normed"), 1)

                qk_inverse(0)
                qk_spread(0)
                qk_inverse(1)
                qk_norm(0)
                qk_spread(1)
                qk_inverse(2)
                qk_norm(1)
                qk_spread(2)
                qk_norm(2)
                dve.wait_ge(S("qk_normed"), 3)
                dve.wait_ge(S("qk_turned"), 1)
                cos = C("ax_cos").unsqueeze(1).broadcast_to([PART, 4, SEQ])
                sin = C("ax_sin").unsqueeze(1).broadcast_to([PART, 4, SEQ])
                for k, (x, bank) in enumerate(((qr[:, :, :], 4), (krt[:, :, 0:SEQ], 0))):
                    t1, t2 = (late[:, 2048 * k + 1024 * i:2048 * k + 1024 * i + 1024].rearrange("p (h t) -> p h t", h=4) for i in range(2))
                    nc.vector.tensor_tensor(t1, x, cos, ALU.mult)
                    link(nc.vector.tensor_tensor(t2, sin, PS[:, bank:bank + 2, :].rearrange("p b (h t) -> p (b h) t", h=2), ALU.mult))
                    ins = nc.vector.tensor_tensor(x, t1, t2, ALU.add)
                ins.then_inc(S("qk_ready"), 1)
                for h in range(MLA_HEADS + 2):
                    if h < MLA_HEADS:
                        c0 = 2 * (h % 2)
                        for t in range(2):
                            c = c0 + t
                            dve.wait_ge(S("s_done"), 2 * h + t + 1)
                            link(nc.vector.reduce_max(ms[:, 4 + c:5 + c], PS[:, SCORE_BANK[h % 2] + t, :], AX.X))
                            nc.vector.tensor_scalar(ms[:, c:c + 1], ms[:, 4 + c:5 + c], -1.0, None, ALU.mult).then_inc(S("neg_max"), 1)
                        for t in range(2):
                            c = c0 + t
                            dve.wait_ge(S("exp_done"), 2 * h + t + 1)
                            link(nc.vector.reciprocal(rstd[:, c:c + 1], root[:, c:c + 1]))
                            nc.vector.tensor_scalar(probs[:, h % 2, t, :], probs[:, h % 2, t, :], rstd[:, c:c + 1], None,
                                                    ALU.mult).then_inc(S("p_ready"), 1)
                    if h >= 2:
                        k = h - 2
                        dve.wait_ge(S("head_hi"), k + 1)
                        nc.vector.tensor_tensor(h_lo[SEQ][:, k, :], PS[:, 4 + k % 2, 0:SEQ], h_hi[SEQ][:, k, :].bitcast(F32),
                                                ALU.subtract).then_inc(S("head_ready"), 1)

            nc.vector.memset(zc0[:, 0:1], 0.0).then_inc(evacuated, 1)
            nc.vector.memset(zc0[:, 1:2], 0.0).then_inc(evacuated, 1)
            for g in range(1, KD // 2):
                add_squares(SEQ, g, 0)
            dve.wait_ge(cond_ready, 1)
            for t in range(ADA_FIRST):
                if t % (ADA_FIRST // 6) == 0:
                    dve.wait_ge(ada_first_in[t // (ADA_FIRST // 6)], 16)
                modulation(t, ada_first[:, t, :], [mod1[:, 0, t:t + 1]], t, bank=0)
                if t == ADA_FIRST - 6:
                    dve.wait_ge(small_in, 96)
                    angles()
                if t >= ADA_FIRST - AHEAD:
                    split_lo(t - ADA_FIRST + AHEAD)
            mods1(0, (0,), 0, 2 * KD)
            for l, ff in enumerate(("dense", "moe")):
                if runs(f"win{l}"):
                    if l == 0:
                        dve.wait_ge(S("trig_ready"), 1)
                    norm(2 * l)
                    mixer(l)
                if runs(ff):
                    norm(2 * l + 1)
                    if ff == "moe":
                        route()
                        dve.wait_ge(S("gates_in"), 1)
                        dve.wait_ge(cond_ready, 2)
                    ffn(ff, lambda t, s: mod1[:, l, 40 + t:41 + t])
                    if ff == "dense":
                        mods1(1, (0,), 0, 30)
                    else:
                        mods2(0, (0,))

            def gate(l, w):
                return lambda t, s: gate2[:, l, w, t, s:s + 1]

            if runs("ffn00"):
                norm(FINAL1)
                dve.wait_ge(ctx_in, 16)
                for g in range(1, KD // 2):
                    add_squares(BOTH, g, NORM_SET[5])
                norm(5)
                ffn("ffn00", gate(0, 0))
                mods2(0, (1, 2))
            if runs("conv_cu"):
                norm(6)
                link(nc.vector.memset(zc[:, :, :, :], 0.0))
                for f in range(KD):
                    q = P0["conv_cu"] + 2 * f
                    split_lo(q + AHEAD)
                    split_lo(q + AHEAD + 1)
                    dve.wait_ge(S("conv_c"), f + 1)
                    nc.vector.tensor_tensor(zc[:, f, :, 1:SEQ + 1], stage_a[:, f % 2, :].rearrange("p (s t) -> p s t", s=2),
                                            PS[:, 2 * (f % 2) + 1, :].rearrange("p (s t) -> p s t", s=2), ALU.mult).then_inc(evacuated, 1)
                dve.wait_ge(evacuated, G0["conv_cu"] + KD)
                for f in range(KD):
                    split_lo(P0["conv_b"] + f + AHEAD)
                    if f % 2 == 0:
                        continue
                    for k in (f - 1, f):
                        t = stage_a[:, k % 2, :].rearrange("p (s t) -> p s t", s=2)
                        link(nc.vector.tensor_scalar(t, zc[:, k, :, 0:SEQ], V("conv", k), None, ALU.mult))
                        for tap in (1, 2):
                            link(nc.vector.scalar_tensor_tensor(out=t, in0=zc[:, k, :, tap:tap + SEQ], scalar=V("conv", KD * tap + k),
                                                                in1=t, op0=ALU.mult, op1=ALU.add))
                        dve.wait_ge(panel_used, USED0 + P0["conv_b"] + k + 1)
                        nc.vector.tensor_tensor(stage_b[:, k % 2, :], stage_a[:, k % 2, :], PS[:, 2 * (k // 2 % 2) + k % 2, :],
                                                ALU.mult).then_inc(S("y_ready"), 1)
                    for k in (f - 1, f):
                        dve.wait_ge(S("y_hi"), k + 1)
                        ins = nc.vector.tensor_tensor(y_lo[:, k, :], stage_b[:, k % 2, :], y_hi[:, k, :].bitcast(F32), ALU.subtract)
                    ins.then_inc(evacuated, 1)
                linear_out("conv_out", BOTH, gate(0, 1))
            if runs("ffn01"):
                norm(7)
                ffn("ffn01", gate(0, 2))
                mods2(1, (0,))
            if runs("ffn10"):
                norm(8)
                ffn("ffn10", gate(1, 0))
                mods2(1, (1, 2))
            if runs("mla"):
                norm(9)
                latent()
            if runs("mla_o"):
                linear_out("mla_o", SEQ, gate(1, 1))
            if runs("ffn11"):
                norm(10)
                ffn("ffn11", gate(1, 2))

        @block.tensor
        def _(pe):
            mm = nc.tensor.matmul

            def passes(o, left, right, start, stop):
                mm(o, left[0], right[0], start=start, stop=False)
                mm(o, left[0], right[1], start=False, stop=False)
                return mm(o, left[1], right[0], start=False, stop=stop)

            def weights(q, tile):
                w = slice(PART * tile, PART * tile + PART)
                return whi[:, q % SLOTS, w], wlo[:, q % SLOTS, w]

            def stay_warm(bank, count):
                for _ in range(count):
                    mm(PS[:, bank, :], ones, C("ret_decay"), start=True, stop=True)

            def norm(n):
                T = NORMS[n][0]
                bank = 0 if n in (1, 3, 7, 10) else 2
                if n not in (0, 5):
                    pe.wait_ge(evacuated, G0[NORM_OF[n]] - 1)
                    stay_warm(bank, T // PART)
                pe.wait_ge(acc_done, 3 * NORM_SET[n] + 3)
                for t in range(T // PART):
                    for c in range(2):
                        ins = mm(PS[:, BC_BANK, SUMS + t:SUMS + t + 1], stage_b[:, c, PART * t:PART * t + PART], ones[:, 0:1],
                                 start=c == 0, stop=c == 1)
                ins.then_inc(sumsq_ready, 1)
                pe.wait_ge(diag_ready, n + 1)
                mm(PS[:, BC_BANK, 0:T], ones, stage_b[:, 1, 0:T], start=True, stop=True).then_inc(bc_ready, 1)
                if n != FINAL1:
                    stay_warm(bank, 2 + T // BOTH)

            def h_chunk(n, k):
                pe.wait_ge(h_ready, KD * modulated(n) + k + 1)

            def first_tiles(n, name, src, tokens):
                p0 = P0[name]
                pe.wait_ge(evacuated, G0[name])
                for k in range(KD):
                    if k % 2 == 0:
                        pe.wait_ge(lo_split, p0 + k // 2 + 1)
                    h_chunk(n, k)
                    for o, T in enumerate(tokens):
                        ins = passes(PS[:, o, 0:T], weights(p0 + k // 2, 4 * (k % 2) + o), (src[0][:, k, 0:T], src[1][:, k, 0:T]),
                                     k == 0, k == KD - 1)
                    if k % 2:
                        ins.then_inc(panel_used, 1)

            def linear(name, n, T, src, first=0):
                p0, g0 = P0[name], G0[name]
                with nc.tensor.Fori(first // 4, n // 4) as i:
                    for j in range(4):
                        if j % 2 == 0:
                            pe.wait_ge(evacuated, g0 + j // 2 - 1 + 2 * i)
                        pe.wait_ge(lo_split, p0 + j + 1 + 4 * i)
                        for k in range(KD):
                            ins = passes(PS[:, j, 0:T], weights(p0 + j, k), (src[0][:, k, 0:T], src[1][:, k, 0:T]),
                                         k == 0, k == KD - 1)
                        ins.then_inc(panel_used, 1)

            def values(name, b):
                p0, g0 = P0[name] + 20, G0[name] + 10
                a = h_hi[SEQ], h_lo[SEQ]
                pe.wait_ge(evacuated, g0 + b - 1)
                for j in range(4):
                    q = p0 + 4 * b + j
                    pe.wait_ge(lo_split, q + 1)
                    for k in (2 * j, 2 * j + 1):
                        w = slice(512 * (k % 2), 512 * (k % 2) + 512)
                        for t in range(2):
                            tok = slice(PART * t, PART * t + PART)
                            ins = passes(PS[:, 2 * b + t, :], (a[0][:, k, tok], a[1][:, k, tok]),
                                         (whi[:, q % SLOTS, w], wlo[:, q % SLOTS, w]), k == 0, k == KD - 1)
                    ins.then_inc(panel_used, 1)

            def ffn(name, norm_of_h):
                e0, n, T, _ = FFN[name]
                p0, g0 = P0[name], G0[name]
                up = 2 * UNITS * KD
                src, hid = (h_hi[T], h_lo[T]), (hid_hi[T], hid_lo[T])
                with nc.tensor.Fori(0, n) as i:
                    for tile in range(EXPERT_PANELS * PANEL):
                        panel, at = divmod(tile, PANEL)
                        if at == 0:
                            pe.wait_ge(lo_split, p0 + panel + 1 + EXPERT_PANELS * i)
                        if tile < 4 * KD:
                            o, k, depth = tile % 4, tile // 4, KD
                            group, bank = o // 2, o % 2
                            if o == 0:
                                h_chunk(norm_of_h, k)
                        elif tile < up:
                            o, k, depth = tile // KD, tile % KD, KD
                            group, bank = o // 2, o % 2
                        else:
                            o, k, depth = (tile - up) // UNITS, (tile - up) % UNITS, UNITS
                            group, bank = UNITS + o // 2, o % 2
                            if o == 0:
                                pe.wait_ge(hid_ready, UNITS * (e0 + i) + k + 1)
                        if k == 0 and bank == 0:
                            pe.wait_ge(evacuated, g0 + group - 2 + EXPERT_GROUPS * i)
                        act_in = src if tile < up else hid
                        ins = passes(PS[:, 2 * (group % 3) + bank, 0:T], weights(p0 + panel, at),
                                     (act_in[0][:, k, 0:T], act_in[1][:, k, 0:T]), k == 0, k == depth - 1)
                        if at == PANEL - 1:
                            ins.then_inc(panel_used, 1)
                        elif tile < up and k == KD - 1 and bank == 1:
                            ins.then_inc(unit_done, 1)

            pe.sem_inc(panel_used, USED0)
            pe.wait_ge(small_in, 96)

            def mixer(l):
                win = f"win{l}"
                prj, val = m["prj"], m["val"]
                first_tiles(2 * l, win, (h_hi[SEQ], h_lo[SEQ]), (SEQ,) * 4)
                for part in (h_hi[SEQ], h_lo[SEQ]):
                    for k in range(KD):
                        ins = mm(PS[0:RANK, 4, 0:SEQ], wga[:, l, k, :], part[:, k, :].bitcast(F32),
                                 start=part is h_hi[SEQ] and k == 0, stop=part is h_lo[SEQ] and k == KD - 1)
                ins.then_inc(S("ga_done"), 1)
                linear(win, 20, SEQ, (h_hi[SEQ], h_lo[SEQ]), first=4)
                values(win, 0)
                pe.wait_ge(S("ga_copied"), l + 1)
                for f in range(2):
                    ins = mm(PS[:, 7, SEQ * f:SEQ * f + SEQ], walpha[:, l, PART * f:PART * f + PART], m["ga"], start=True, stop=True)
                ins.then_inc(S("z_done"), 1)
                values(win, 1)
                pe.wait_ge(evacuated, G0[win] + 12)
                for b in range(4):
                    ins = mm(PS[:, b, :], C("turn"), prj[:, 4 + 2 * b:6 + 2 * b, :].rearrange("p a t -> p (a t)"), start=True, stop=True)
                ins.then_inc(S("turned"), 1)
                pe.wait_ge(S("rotated"), l + 1)
                for j in range(2):
                    tok = slice(PART * j, PART * j + PART)
                    for h in range(HEADS):
                        ins = mm(PS[:, 4 + j, PART * h:PART * h + PART], prj[:, 8 + h, tok], prj[:, 4 + h, tok], start=True, stop=True)
                ins.then_inc(S("ret_scores"), 1)
                for j in range(2):
                    for h in range(HEADS):
                        ins = nc.tensor.transpose(PS[:, j, PART * h:PART * h + PART], prj[:, 8 + h, PART * j:PART * j + PART], ident)
                ins.then_inc(S("ret_kt"), 1)
                pe.wait_ge(S("gla_qk"), l + 1)
                pe.wait_ge(S("sr_ready"), l + 1)
                for j in range(2):
                    tok = slice(PART * j, PART * j + PART)
                    for h in range(HEADS):
                        r = slice(64 * (h % 2), 64 * (h % 2) + 64)
                        for way, (kk, qq) in enumerate(((prj[:, 2:4, :], prj[:, 0:2, :]), (m["kb"], m["qb"]))):
                            at = PART * (2 * way + h // 2)
                            ins = mm(PS[:, 2 + 2 * j + h % 2, at:at + PART], kk[r, h // 2, tok], qq[r, h // 2, tok], start=True, stop=True)
                ins.then_inc(S("gla_scores"), 1)
                for f in range(2):
                    for j in range(2):
                        ins = nc.tensor.transpose(PS[:, 7, PART * (2 * f + j):PART * (2 * f + j) + PART],
                                                  m["kd"][:, f, PART * j:PART * j + PART], ident)
                ins.then_inc(S("kd_turned"), 1)
                pe.wait_ge(S("kdt_ready"), l + 1)
                pe.wait_ge(S("kdr_ready"), l + 1)
                for c, bank in enumerate((0, 1, 7)):
                    r, j = slice(64 * (c % 2), 64 * (c % 2) + 64), c // 2
                    for f in range(2):
                        ins = mm(PS[:, bank, 256 * f:256 * f + 256], m["kdt"][r, 2 * f + j, :], val[r, j, 256 * f:256 * f + 256],
                                 start=True, stop=True)
                ins.then_inc(S("gla_upd"), 1)
                pe.wait_ge(S("sc_ready"), l + 1)
                for c, bank in enumerate((2, 3, 4)):
                    r, j = slice(64 * (c % 2), 64 * (c % 2) + 64), c // 2
                    for h in range(HEADS):
                        w = slice(PART * h, PART * h + PART)
                        ins = mm(PS[:, bank, w], m["kdr"][r, j, w], val[r, j, 512 + PART * h:512 + PART * h + PART], start=True, stop=True)
                ins.then_inc(S("ret_upd"), 1)
                for h in range(2 * HEADS):
                    if h == 0:
                        pe.wait_ge(S("gs_ready"), l + 1)
                    if h == HEADS:
                        pe.wait_ge(S("rs_ready"), l + 1)
                        pe.wait_ge(S("qd_ready"), l + 1)
                    g, hh = divmod(h, HEADS)
                    for j in range(2):
                        w = slice(PART * hh, PART * hh + PART)
                        at = SEQ * (h % 2) + PART * j
                        mm(PS[:, h // 2, at:at + PART], val[:, j, PART * h:PART * h + PART], (m["sr"] if g else m["sc"])[:, j, w],
                           start=True, stop=False, skip_group_check=True)
                        for c in (2 * j, 2 * j + 1):
                            if c == 0:
                                continue
                            tok = slice(CHUNK * c, CHUNK * c + CHUNK)
                            state, q = ((m["rs"][:, c - 1, w], prj[:, 4 + hh, tok]) if g else
                                        (m["gs"][:, c - 1, hh, :], prj[:, hh // 2, tok]))
                            ins = mm(PS[:, h // 2, at + CHUNK * (c % 2):at + CHUNK * (c % 2) + CHUNK], state, q,
                                     start=False, stop=c % 2 == 1, skip_group_check=True)
                ins.then_inc(S("o_done"), 1)
                pe.wait_ge(S("o_copied"), l + 1)
                for b in range(2):
                    ins = mm(PS[:, 4 + b, :], ones, m["o"][:, 4 + 2 * b:6 + 2 * b, :].rearrange("p a t -> p (a t)"), start=True, stop=True)
                ins.then_inc(S("mean_done"), 1)
                stay_warm(0, 4)
                pe.wait_ge(S("osq_ready"), l + 1)
                for h in range(2 * HEADS):
                    for j in range(2):
                        ins = mm(PS[:, 7, 2 * h + j:2 * h + j + 1], m["osq"][:, h, PART * j:PART * j + PART], ones[:, 0:1], start=True, stop=True)
                ins.then_inc(S("o_sums"), 1)
                pe.wait_ge(S("odiag_ready"), l + 1)
                for b in range(4):
                    ins = mm(PS[:, b, :], ones, m["odiag"][:, 4 * b:4 * b + 4, :].rearrange("p a t -> p (a t)"), start=True, stop=True)
                ins.then_inc(S("o_spread"), 1)
                stay_warm(4, 8)
                pe.wait_ge(S("o_ready"), l + 1)
                linear(f"wout{l}", 8, SEQ, (h_hi[SEQ], h_lo[SEQ]))

            def route():
                for k in range(KD):
                    h_chunk(3, k)
                    for t in range(2):
                        for part in (h_hi[SEQ], h_lo[SEQ]):
                            ins = mm(PS[:, 5 + t, 0:N_EXPERTS], part[:, k, PART * t:PART * t + PART].bitcast(F32), wroute[:, k, :],
                                     start=part is h_hi[SEQ] and k == 0, stop=part is h_lo[SEQ] and k == KD - 1)
                ins.then_inc(S("logits"), 1)
                for t in range(2):
                    pe.wait_ge(S("gdiag_ready"), t + 1)
                    for b in range(2):
                        ins = mm(PS[:, 2 * t + b, :], ones, gdiag[:, t, 4 * b:4 * b + 4, :].rearrange("p e t -> p (e t)"), start=True, stop=True)
                    ins.then_inc(S("gates_spread"), 1)
                pe.wait_ge(S("gates_in"), 1)

            for l, ff in enumerate(("dense", "moe")):
                if runs(f"win{l}"):
                    norm(2 * l)
                    mixer(l)
                if runs(ff):
                    norm(2 * l + 1)
                    if ff == "moe":
                        route()
                    ffn(ff, 2 * l + 1)
            if runs("ffn00"):
                norm(FINAL1)
                norm(5)
                ffn("ffn00", 5)
            if runs("conv_cu"):
                norm(6)
                first_tiles(6, "conv_cu", (h_hi[BOTH], h_lo[BOTH]), (BOTH,) * 4)
                linear("conv_cu", 16, BOTH, (h_hi[BOTH], h_lo[BOTH]), first=4)
                linear("conv_b", 8, BOTH, (h_hi[BOTH], h_lo[BOTH]))
                pe.wait_ge(evacuated, G0["conv_b"] + 4)
                linear("conv_out", 8, BOTH, (y_hi, y_lo))
            for n, name in ((7, "ffn01"), (8, "ffn10")):
                if runs(name):
                    norm(n)
                    ffn(name, n)

            def latent():
                p0, g0 = P0["mla"], G0["mla"]
                first_tiles(9, "mla", (h_hi[BOTH], h_lo[BOTH]), (SEQ, SEQ, BOTH, BOTH))
                pe.wait_ge(S("lat_sq"), 1)
                for t in range(2):
                    for f in range(2):
                        mm(PS[:, BC_BANK, SUMS + t:SUMS + t + 1], late[:, SEQ * f + PART * t:SEQ * f + PART * t + PART], ones[:, 0:1],
                           start=f == 0, stop=f == 1)
                for t in range(4):
                    ins = mm(PS[:, BC_BANK, SUMS + 2 + t:SUMS + 3 + t], late[:, 512 + PART * t:512 + PART * t + PART], ones[:, 0:1],
                             start=True, stop=True)
                ins.then_inc(S("lat_sum"), 1)
                pe.wait_ge(S("lat_diag"), 1)
                mm(PS[:, 4, 0:SEQ], ones, late[:, 1024:1280], start=True, stop=True)
                mm(PS[:, 5, :], ones, late[:, 1280:1792], start=True, stop=True).then_inc(S("lat_bc"), 1)
                pe.wait_ge(S("lat_ready"), 1)
                for j in range(3):
                    g = 2 + j
                    pe.wait_ge(lo_split, p0 + 4 + j + 1)
                    pe.wait_ge(evacuated, g0 + g - 2)
                    for o in range(4):
                        for k in range(2):
                            ins = passes(PS[:, 2 * (g % 3) + o // 2, SEQ * (o % 2):SEQ * (o % 2) + SEQ], weights(p0 + 4 + j, 2 * o + k),
                                         (cq_hi[:, k, :], cq_lo[:, k, :]), k == 0, k == 1)
                    ins.then_inc(panel_used, 1)
                pe.wait_ge(lo_split, p0 + 8)
                for h in range(MLA_HEADS):
                    g = 5 + h // 2
                    if h % 2 == 0:
                        pe.wait_ge(evacuated, g0 + g - 2)
                    ins = passes(PS[:, 2 * (g % 3) + h % 2, :], weights(p0 + 7, h), (ckv_hi[:, :], ckv_lo[:, :]), True, True)
                    if h == MLA_HEADS - 1:
                        ins.then_inc(panel_used, 1)
                    elif h % 2:
                        ins.then_inc(group_done, 1)
                halfs = C("low")[:, 0:1], C("high")[:, 0:1]
                squares = late[:, 0:2048]

                def sums(r):
                    pe.wait_ge(S("qk_sq"), r + 1)
                    for i in range(16):
                        tok = slice(PART * i, PART * i + PART)
                        if r:
                            ins = mm(PS[:, 5 + r, 16 + i:17 + i], squares[:, tok], ones[:, 0:1], start=True, stop=True)
                            continue
                        o = PS[:, 7, i:i + 1]
                        at = SEQ * (i // 4) + PART * (i % 2)
                        qs = stage_a[:, :, :].rearrange("p a b -> p (a b)")[:, at:at + PART]
                        mm(o, squares[:, tok], ones[:, 0:1], start=True, stop=False)
                        mm(o, qs, halfs[i // 2 % 2], start=False, stop=True)
                    if r == 0:
                        for t in range(4):
                            ins = mm(PS[:, 7, 32 + t:33 + t], stage_b[:, 1, PART * t:PART * t + PART], halfs[0], start=True, stop=True)
                    ins.then_inc(S("qk_sum"), 1)

                def repeat(r):
                    pe.wait_ge(S("qk_diag"), r + 1)
                    if r:
                        pe.wait_ge(S("qk_normed"), r)
                    for b in range(4):
                        ins = mm(PS[:, b, :], ones, late[:, 2048 + 512 * b:2560 + 512 * b], start=True, stop=True)
                    ins.then_inc(S("qk_bc"), 1)

                sums(0)
                pe.wait_ge(lo_split, p0 + 9)
                for t in range(4):
                    g = 9 + t
                    tok = slice(PART * t, PART * t + PART)
                    pe.wait_ge(evacuated, g0 + g - 2)
                    for b in range(2):
                        w = slice(512 * b, 512 * b + 512)
                        q = (p0 + 8) % SLOTS
                        ins = passes(PS[:, 2 * (g % 3) + b, :], (ckv_hi[:, tok], ckv_lo[:, tok]), (whi[:, q, w], wlo[:, q, w]), True, True)
                    ins.then_inc(panel_used if t == 3 else group_done, 1)
                sums(1)
                pe.wait_ge(evacuated, g0 + 13)
                repeat(0)
                sums(2)
                repeat(1)
                repeat(2)
                pe.wait_ge(S("qk_normed"), 3)
                for b in range(2):
                    mm(PS[:, 4 + b, :], C("ax_turn"), qr[:, 2 * b:2 * b + 2, :].rearrange("p a t -> p (a t)"), start=True, stop=True)
                for b in range(2):
                    ins = mm(PS[:, b, :], C("ax_turn"), krt[:, 2 * b:2 * b + 2, 0:SEQ], start=True, stop=True)
                ins.then_inc(S("qk_turned"), 1)
                pe.wait_ge(S("qk_ready"), 1)
                qn = X[:, :, SEQ:BOTH]

                def scores(h):
                    r = slice(64 * (h % 2), 64 * (h % 2) + 64)
                    for t in range(2):
                        tok, o = slice(PART * t, PART * t + PART), PS[:, SCORE_BANK[h % 2] + t, :]
                        if h >= 2:
                            pe.wait_ge(S("exp_done"), 2 * h + t - 3)
                        mm(o, qn[:, h, tok], kn[:, h, :], start=True, stop=False)
                        mm(o, qr[r, h // 2, tok], krt[r, h // 2, :], start=False, stop=True).then_inc(S("s_done"), 1)

                def outputs(h):
                    pe.wait_ge(S("pt_copied"), 2 * h + 2)
                    if h >= 2:
                        pe.wait_ge(S("head_ready"), h - 1)
                    for k in range(4):
                        ins = mm(PS[:, 4 + h % 2, 0:SEQ], val2[:, k, PART * h:PART * h + PART], pts[:, h % 2, k, :], start=k == 0, stop=k == 3)
                    ins.then_inc(S("head_done"), 1)

                scores(0)
                for h in range(MLA_HEADS):
                    if h + 1 < MLA_HEADS:
                        scores(h + 1)
                    for t in range(2):
                        pe.wait_ge(S("p_ready"), 2 * h + t + 1)
                        if h:
                            pe.wait_ge(S("pt_copied"), 2 * h - 1 + t)
                        for k in range(4):
                            ins = nc.tensor.transpose(PS[:, 2 + t, PART * k:PART * k + PART], probs[:, h % 2, t, PART * k:PART * k + PART], ident)
                        ins.then_inc(S("p_turned"), 1)
                    if h:
                        outputs(h - 1)
                outputs(MLA_HEADS - 1)

            if runs("mla"):
                norm(9)
                latent()
            if runs("mla_o"):
                pe.wait_ge(S("head_ready"), MLA_HEADS)
                linear("mla_o", 8, SEQ, (h_hi[SEQ], h_lo[SEQ]))
            if runs("ffn11"):
                norm(10)
                ffn("ffn11", 10)


def tiles(w, n=PART):
    k, cols = w.shape
    return w.reshape(k // PART, PART, cols // n, n).transpose(1, 2, 0, 3)


def panels(blocks, per):
    p = blocks.shape[0]
    flat = blocks.reshape(p, -1, per * PART).transpose(1, 0, 2)
    out = np.zeros((flat.shape[0], p, PANEL * PART), np.float32)
    out[:, :, :per * PART] = flat
    return out


def k_major(blocks):
    first = blocks[:, :4].transpose(0, 2, 1, 3).reshape(PART, 4, KD, PART)
    return np.concatenate([first, blocks[:, 4:]], axis=1)


def columns(v):
    return np.ascontiguousarray(np.asarray(v).reshape(-1, PART).T)


def expert(w1, w3, w2):
    up = np.stack([tiles(w1), tiles(w3)], axis=2).reshape(PART, -1, KD, PART)
    return np.concatenate([panels(k_major(up), PANEL), panels(tiles(w2), PANEL)])


def lay_out(i):
    out = []
    for l in range(2):
        w = i["w_in"][l]
        gq, gk, gv, gr, _, rq, rk, rv, rg = np.split(w, np.cumsum([256, 256, 512, 512, RANK, 512, 512, 512]), axis=1)
        out.append(panels(k_major(tiles(np.concatenate([gq, gk, rq, rk, gr, rg], axis=1))), KD))
        out.append(panels(tiles(np.concatenate([gv, rv], axis=1), 512), KD))
        out.append(panels(tiles(i["w_out"][l]), KD))
        if l == 0:
            for f in range(2):
                s = slice(HALF_F * f, HALF_F * f + HALF_F)
                out.append(expert(i["ffn_w1"][0][:, s], i["ffn_w3"][0][:, s], i["ffn_w2"][0][s]))
        else:
            for e in range(N_EXPERTS):
                out.append(expert(i["moe_w1"][0, e], i["moe_w3"][0, e], i["moe_w2"][0, e]))

    def ffn(l, k):
        for f in range(2):
            s = slice(HALF_F * f, HALF_F * f + HALF_F)
            out.append(expert(i["ffn_w1_2"][l, k][:, s], i["ffn_w3_2"][l, k][:, s], i["ffn_w2_2"][l, k][s]))

    ffn(0, 0)
    b, c, u = (tiles(x) for x in np.split(i["sc_w_in_2"][0], 3, axis=1))
    out.append(panels(k_major(np.stack([c, u], axis=2).reshape(PART, -1, KD, PART)), KD))
    out.append(panels(b, KD))
    out.append(panels(tiles(i["sc_w_out_2"][0]), KD))
    ffn(0, 1)
    ffn(1, 0)
    wa = i["mla_w_a_2"][0]
    out.append(panels(k_major(tiles(np.concatenate([wa, wa[:, Q_LORA + PART:]], axis=1))), KD))
    uq = i["mla_w_uq_2"][0].reshape(Q_LORA, MLA_HEADS, QK_HEAD)
    uq = np.concatenate([uq[:, :, :PART].reshape(Q_LORA, -1), uq[:, :, PART:].reshape(Q_LORA, -1)], axis=1)
    out.append(panels(tiles(uq), KD))
    ukv = i["mla_w_ukv_2"][0].reshape(PART, MLA_HEADS, 2, PART)
    out.append(panels(tiles(np.concatenate([ukv[:, :, 0].reshape(PART, -1), ukv[:, :, 1].reshape(PART, -1)], axis=1)), KD))
    out.append(panels(tiles(i["mla_w_o_2"][0]), KD))
    ffn(1, 1)
    w = np.concatenate(out)
    assert len(w) == P0["end"]
    wstream = np.concatenate([w, np.zeros((PANELS - len(w), PART, PANEL * PART), np.float32)])

    def ada_panels(w):
        return w.T.reshape(-1, PART, D)

    adastream = np.concatenate([ada_panels(i["ada_w"][0]), ada_panels(i["ada_w"][1]),
                                ada_panels(i["w_mod_2"][0]), ada_panels(i["w_mod_2"][1])])
    g_q, g_k = i["mla_g_q_2"][0], i["mla_g_k_2"][0]
    c_rows = np.broadcast_to(np.stack([i["c"][0], i["c_2"][0], i["c_ctx_2"]]), (PART, 3, D))
    parts = {"mix_g": i["norm_mix_g"], "ffn_g": i["norm_ffn_g"],
             "ada_b": i["ada_b"], "mod_b": i["b_mod_2"], "g2": i["g_norm_2"], "alpha_b": i["gla_b_alpha"], "gla_g": i["gla_norm_g"],
             "gn_g": i["ret_gn_g"], "gn_b": i["ret_gn_b"], "final_g": i["final_g"], "conv": i["sc_conv_2"][0],
             "qa_g": i["mla_g_qa_2"], "kva_g": i["mla_g_kva_2"],
             "q_g": np.concatenate([g_q, g_q[PART:]]), "k_g": np.concatenate([g_k, g_k[PART:]])}
    vecs = np.concatenate([columns(parts[n]) for n in VEC], axis=1)
    consts = np.concatenate(list(constants().values()), axis=1)

    def major(x):
        return np.ascontiguousarray(x.T.reshape(KD, PART, -1).transpose(1, 0, 2))

    s = 2 * 256 + 2 * 512
    ga = i["w_in"][:, :, s:s + RANK].reshape(2, KD, PART, RANK).transpose(2, 0, 1, 3)
    return {
        "wstream": wstream, "adastream": adastream, "c_rows": np.ascontiguousarray(c_rows), "vecs": vecs, "consts": consts,
        "xT": major(i["x"][0]), "ctxT": major(i["ctx_2"][0]),
        "pos": np.ascontiguousarray(np.broadcast_to(i["positions"], (PART, SEQ))),
        "w_ga": np.ascontiguousarray(ga),
        "w_alpha": np.ascontiguousarray(i["gla_w_alpha"].transpose(1, 0, 2)),
        "router": np.ascontiguousarray(i["router_w"][0].reshape(KD, PART, N_EXPERTS).transpose(1, 0, 2)),
    }


LAST = "end"


def kernel(**inputs):
    import concourse.bacc as bacc
    from concourse.bass_utils import run_bass_kernel_spmd

    nc = bacc.Bacc("TRN2", target_bir_lowering=False, num_devices=1)
    arrays = {f"in_{n}": a for n, a in lay_out({n: np.asarray(a) for n, a in inputs.items()}).items()}
    args = {n[3:]: nc.dram_tensor(n, a.shape, mybir.dt.from_np(a.dtype), kind="ExternalInput").ap() for n, a in arrays.items()}
    out = nc.dram_tensor("out_x", (PART, KD, SEQ), F32, kind="ExternalOutput").ap()
    build(nc, out=out, last=LAST, **args)
    r = run_bass_kernel_spmd(nc, [arrays], core_ids=[0])
    y = r.results[0]["out_x"]
    return np.ascontiguousarray(y.transpose(1, 0, 2).reshape(D, SEQ).T)[None]
```
